# Optimizing a Trainium2 kernel written in Bass

```python
import math
import jax, jax.numpy as jnp
from jax import lax
import numpy as np

D_MODEL = 1024
BATCH = 1
SEQ = 128
DEPTH = 4
DEC_BATCH = 1
DEC_SEQ = 512
PAST_LEN = 128

GRID_W = 64
N_MIXERS = 3
N_GQA_LAYERS = (DEPTH + 2) // 3
N_DIFF_LAYERS = (DEPTH + 1) // 3
N_MLSTM_LAYERS = DEPTH // 3

HEAD_DIM = 64
Q_BLOCK = 128
ROPE_THETA = 10000.0
NORM_EPS = 1e-6

GQA_HEADS = 16
GQA_KV_HEADS = 4
GQA_GROUP = GQA_HEADS // GQA_KV_HEADS
GQA_Q_W = GQA_HEADS * HEAD_DIM
GQA_KV_W = GQA_KV_HEADS * HEAD_DIM
GQA_BRANCH = GQA_Q_W
GQA_IN = GQA_Q_W + 2 * GQA_KV_W + GQA_BRANCH

DIFF_HEADS = 8
DIFF_QK_W = DIFF_HEADS * 2 * HEAD_DIM
DIFF_V_DIM = 2 * HEAD_DIM
DIFF_BRANCH = DIFF_HEADS * DIFF_V_DIM
DIFF_IN = 2 * DIFF_QK_W + 2 * DIFF_BRANCH

MLSTM_INNER = 2 * D_MODEL
MLSTM_HEADS = 4
MLSTM_HEAD_DIM = MLSTM_INNER // MLSTM_HEADS
MLSTM_QKV_BLOCK = 4
MLSTM_N_BLOCKS = MLSTM_INNER // MLSTM_QKV_BLOCK
MLSTM_CONV_K = 4
MLSTM_CHUNK = 64
MLSTM_IN = 2 * MLSTM_INNER

kernel_name = "hybrid_diffusion_gqa_diff_mlstm_step"

def rms_norm(x, g, eps=NORM_EPS):
    xf = x.astype(jnp.float32)
    y = xf * lax.rsqrt(jnp.mean(xf * xf, axis=-1, keepdims=True) + eps)
    return (y * g.astype(jnp.float32)).astype(x.dtype)

def adaln(cond, w_mod, b_mod):
    mod = jax.nn.silu(cond) @ w_mod + b_mod
    mod = mod.reshape(-1, 1, 3 * D_MODEL)
    return jnp.split(mod, 3, axis=-1)

def axial_rope_tables(rows):
    t = jnp.arange(rows * GRID_W)
    row = (t // GRID_W).astype(jnp.float32)
    col = (t % GRID_W).astype(jnp.float32)
    n_freq = HEAD_DIM // 4
    inv = ROPE_THETA ** (-jnp.arange(n_freq, dtype=jnp.float32) / n_freq)
    ang = jnp.concatenate([row[:, None] * inv, col[:, None] * inv], axis=-1)
    return jnp.cos(ang), jnp.sin(ang)

def apply_rope(x, cos, sin):
    shp = (1, x.shape[1]) + (1,) * (x.ndim - 3) + (cos.shape[-1],)
    c = cos.reshape(shp)
    s = sin.reshape(shp)
    xf = x.astype(jnp.float32)
    x1, x2 = jnp.split(xf, 2, axis=-1)
    return jnp.concatenate([x1 * c - x2 * s, x2 * c + x1 * s], axis=-1).astype(x.dtype)

def map_query_blocks(fn, q):
    B, S = q.shape[:2]
    nb = S // Q_BLOCK
    qb = jnp.moveaxis(q.reshape((B, nb, Q_BLOCK) + q.shape[2:]), 1, 0)
    o = lax.map(fn, qb)
    return jnp.moveaxis(o, 0, 1).reshape((B, S) + o.shape[3:])

def gated_out(o, z, w_out):
    B, S = z.shape[:2]
    return (o.reshape(B, S, -1) * jax.nn.silu(z)) @ w_out

def gqa_attention(q, k, v):
    scale = HEAD_DIM ** -0.5

    def block(qb):
        s = jnp.einsum('bqhgd,bkhd->bhgqk', qb, k).astype(jnp.float32) * scale
        p = jax.nn.softmax(s, axis=-1).astype(v.dtype)
        return jnp.einsum('bhgqk,bkhd->bqhgd', p, v)

    return map_query_blocks(block, q)

def gqa_project(h, w_in, q_g, k_g):
    B, S, _ = h.shape
    q, k, v, z = jnp.split(h @ w_in, [GQA_Q_W, GQA_Q_W + GQA_KV_W, GQA_Q_W + 2 * GQA_KV_W], axis=-1)
    q = rms_norm(q.reshape(B, S, GQA_KV_HEADS, GQA_GROUP, HEAD_DIM), q_g)
    k = rms_norm(k.reshape(B, S, GQA_KV_HEADS, HEAD_DIM), k_g)
    return q, k, v.reshape(B, S, GQA_KV_HEADS, HEAD_DIM), z

def gqa_context(h, w_in, q_g, k_g, w_out):
    q, k, v, z = gqa_project(h, w_in, q_g, k_g)
    return gated_out(gqa_attention(q, k, v), z, w_out), k, v

def gqa_latent(h, k_ctx, v_ctx, cos, sin, w_in, q_g, k_g, w_out):
    q, k, v, z = gqa_project(h, w_in, q_g, k_g)
    q = apply_rope(q, cos, sin)
    k = apply_rope(k, cos, sin)
    k_all = jnp.concatenate([k, k_ctx.astype(k.dtype)], axis=1)
    v_all = jnp.concatenate([v, v_ctx.astype(v.dtype)], axis=1)
    return gated_out(gqa_attention(q, k_all, v_all), z, w_out)

def diff_lambda_init(layer_idx):
    return 0.8 - 0.6 * math.exp(-0.3 * layer_idx)

def diff_lambda(lq1, lk1, lq2, lk2, lam_init):
    f = lambda a: a.astype(jnp.float32)
    return jnp.exp(jnp.sum(f(lq1) * f(lk1))) - jnp.exp(jnp.sum(f(lq2) * f(lk2))) + lam_init

def diff_attention(q, k, v, lam):
    scale = HEAD_DIM ** -0.5

    def block(qb):
        s = jnp.einsum('bqhjd,bkhjd->bhjqk', qb, k).astype(jnp.float32) * scale
        p = jax.nn.softmax(s, axis=-1)
        a = (p[:, :, 0] - lam * p[:, :, 1]).astype(v.dtype)
        return jnp.einsum('bhqk,bkhe->bqhe', a, v)

    return map_query_blocks(block, q)

def diff_project(h, w_in):
    B, S, _ = h.shape
    q, k, v, z = jnp.split(h @ w_in, [DIFF_QK_W, 2 * DIFF_QK_W, 2 * DIFF_QK_W + DIFF_BRANCH], axis=-1)
    shp = (B, S, DIFF_HEADS, 2, HEAD_DIM)
    return q.reshape(shp), k.reshape(shp), v.reshape(B, S, DIFF_HEADS, DIFF_V_DIM), z

def diff_out(o, z, subln_g, lam_init, w_out):
    o = rms_norm(o, subln_g) * (1.0 - lam_init)
    return gated_out(o, z, w_out)

def diff_context(h, lam, lam_init, w_in, subln_g, w_out):
    q, k, v, z = diff_project(h, w_in)
    return diff_out(diff_attention(q, k, v, lam), z, subln_g, lam_init, w_out), k, v

def diff_latent(h, k_ctx, v_ctx, cos, sin, lam, lam_init, w_in, subln_g, w_out):
    q, k, v, z = diff_project(h, w_in)
    q = apply_rope(q, cos, sin)
    k = apply_rope(k, cos, sin)
    k_all = jnp.concatenate([k, k_ctx.astype(k.dtype)], axis=1)
    v_all = jnp.concatenate([v, v_ctx.astype(v.dtype)], axis=1)
    return diff_out(diff_attention(q, k_all, v_all, lam), z, subln_g, lam_init, w_out)

def short_conv(x, w, b):
    pad_l = MLSTM_CONV_K // 2
    y = lax.conv_general_dilated(x, w[:, None, :].astype(x.dtype), window_strides=(1,),
                                 padding=[(pad_l, MLSTM_CONV_K - 1 - pad_l)],
                                 dimension_numbers=('NWC', 'WIO', 'NWC'),
                                 feature_group_count=x.shape[-1])
    return y + b

def headwise(x, w):
    B, S, _ = x.shape
    y = jnp.einsum('bsnc,ncd->bsnd', x.reshape(B, S, MLSTM_N_BLOCKS, MLSTM_QKV_BLOCK), w)
    return y.reshape(B, S, MLSTM_INNER)

def mlstm_scan(q, k, v, i_pre, f_pre, C0, n0, m0):
    B, S, H, DH = q.shape
    L = MLSTM_CHUNK
    nc = S // L

    def chunks(a):
        a = a.astype(jnp.float32).reshape((B, nc, L, H) + a.shape[3:])
        return jnp.moveaxis(jnp.moveaxis(a, 1, 0), 3, 2)

    tril = jnp.tril(jnp.ones((L, L), dtype=bool))

    def step(carry, inp):
        C, n, m = carry
        qc, kc, vc, ic, fc = inp
        b = jnp.cumsum(jax.nn.log_sigmoid(fc), axis=-1)
        dmat = jnp.where(tril, b[..., :, None] - b[..., None, :] + ic[..., None, :], -jnp.inf)
        inter = b + m[..., None]
        m_t = jnp.maximum(jnp.max(dmat, axis=-1), inter)
        s = jnp.einsum('bhtd,bhsd->bhts', qc, kc) * jnp.exp(dmat - m_t[..., None])
        w_inter = jnp.exp(inter - m_t)
        num = jnp.einsum('bhts,bhse->bhte', s, vc) + w_inter[..., None] * jnp.einsum('bhtd,bhde->bhte', qc, C)
        den = jnp.sum(s, axis=-1) + w_inter * jnp.einsum('bhtd,bhd->bht', qc, n)
        h = num / jnp.maximum(jnp.abs(den), jnp.exp(-m_t))[..., None]
        g_s = b[..., -1:] - b + ic
        m_new = jnp.maximum(b[..., -1] + m, jnp.max(g_s, axis=-1))
        decay = jnp.exp(b[..., -1] + m - m_new)
        kw = kc * jnp.exp(g_s - m_new[..., None])[..., None]
        C_new = decay[..., None, None] * C + jnp.einsum('bhsd,bhse->bhde', kw, vc)
        n_new = decay[..., None] * n + jnp.sum(kw, axis=2)
        return (C_new, n_new, m_new), h

    init = (C0.astype(jnp.float32), n0.astype(jnp.float32), m0.astype(jnp.float32))
    (C, n, m), h = lax.scan(step, init, (chunks(q), chunks(k), chunks(v), chunks(i_pre), chunks(f_pre)))
    h = jnp.moveaxis(jnp.moveaxis(h, 2, 3), 0, 1).reshape(B, S, H, DH)
    return h.astype(q.dtype), C, n, m

def mlstm_bidir(q, k, v, g_f, g_b, C0, n0, m0):
    H = MLSTM_HEADS
    rev = lambda a: jnp.flip(a, axis=1)
    h_f, Cf, nf, mf = mlstm_scan(q, k, v, g_f[..., :H], g_f[..., H:], C0[:, 0], n0[:, 0], m0[:, 0])
    h_b, Cb, nb, mb = mlstm_scan(rev(q), rev(k), rev(v), rev(g_b[..., :H]), rev(g_b[..., H:]),
                                 C0[:, 1], n0[:, 1], m0[:, 1])
    h = h_f + rev(h_b)
    return h, jnp.stack([Cf, Cb], axis=1), jnp.stack([nf, nb], axis=1), jnp.stack([mf, mb], axis=1)

def mlstm_mixer(h, C0, n0, m0, w_in, conv_w, conv_b, w_q, w_k, w_v, w_gf, b_gf, w_gb, b_gb, mh_g, skip, w_out):
    B, S, _ = h.shape
    x_m, z = jnp.split(h @ w_in, 2, axis=-1)
    x_c = jax.nn.silu(short_conv(x_m, conv_w, conv_b))
    q = headwise(x_c, w_q)
    k = headwise(x_c, w_k)
    v = headwise(x_m, w_v)
    g_in = jnp.concatenate([q, k, v], axis=-1)
    g_f = g_in @ w_gf + b_gf
    g_b = g_in @ w_gb + b_gb
    heads = lambda a: a.reshape(B, S, MLSTM_HEADS, MLSTM_HEAD_DIM)
    hh, C, n, m = mlstm_bidir(heads(q), heads(k * (MLSTM_HEAD_DIM ** -0.5)), heads(v), g_f, g_b, C0, n0, m0)
    hf = hh.astype(jnp.float32)
    mu = jnp.mean(hf, axis=-1, keepdims=True)
    var = jnp.mean(jnp.square(hf - mu), axis=-1, keepdims=True)
    hn = ((hf - mu) * lax.rsqrt(var + NORM_EPS)).reshape(B, S, MLSTM_INNER) * mh_g.astype(jnp.float32)
    y = (hn.astype(h.dtype) + skip * x_c) * jax.nn.silu(z)
    return y @ w_out, C, n, m

def setup_inputs(seed: int = 0) -> dict:
    key = jax.random.key(seed)
    ks = iter(jax.random.split(key, 64))
    nrm = lambda shape, scale: scale * jax.random.normal(next(ks), shape, jnp.float32)
    D = D_MODEL
    H, DH = MLSTM_HEADS, MLSTM_HEAD_DIM
    NG, ND, NM = N_GQA_LAYERS, N_DIFF_LAYERS, N_MLSTM_LAYERS
    gate_in = 3 * MLSTM_INNER

    def gate_bias():
        return jnp.concatenate([nrm((NM, H), 0.1), jnp.linspace(3.0, 6.0, H)[None, :] + nrm((NM, H), 0.1)], axis=-1)

    inputs = {}
    inputs["x_prompt"] = nrm((BATCH, SEQ, D), 1.0)
    inputs["x_sample"] = nrm((DEC_BATCH, DEC_SEQ, D), 1.0)
    inputs["cache_gqa_k"] = nrm((DEC_BATCH, NG, PAST_LEN, GQA_KV_HEADS, HEAD_DIM), 1.0)
    inputs["cache_gqa_v"] = nrm((DEC_BATCH, NG, PAST_LEN, GQA_KV_HEADS, HEAD_DIM), 1.0)
    inputs["cache_diff_k"] = nrm((DEC_BATCH, ND, PAST_LEN, DIFF_HEADS, 2, HEAD_DIM), 1.0)
    inputs["cache_diff_v"] = nrm((DEC_BATCH, ND, PAST_LEN, DIFF_HEADS, DIFF_V_DIM), 1.0)
    inputs["state_mlstm_C"] = nrm((DEC_BATCH, NM, 2, H, DH, DH), 0.05)
    inputs["state_mlstm_n"] = nrm((DEC_BATCH, NM, 2, H, DH), 0.05)
    inputs["state_mlstm_m"] = 1.0 + nrm((DEC_BATCH, NM, 2, H), 0.5)
    inputs["c"] = nrm((DEC_BATCH, D), 1.0)
    inputs["c_ctx"] = nrm((D,), 1.0)
    inputs["norm_g"] = 1.0 + nrm((DEPTH, D), 0.02)
    inputs["w_mod"] = nrm((DEPTH, D, 3 * D), 0.5 * D ** -0.5)
    inputs["b_mod"] = nrm((DEPTH, 3 * D), 0.02)
    inputs["gqa_w_in"] = nrm((NG, D, GQA_IN), D ** -0.5)
    inputs["gqa_q_norm_g"] = 1.0 + nrm((NG, HEAD_DIM), 0.02)
    inputs["gqa_k_norm_g"] = 1.0 + nrm((NG, HEAD_DIM), 0.02)
    inputs["gqa_w_out"] = nrm((NG, GQA_BRANCH, D), GQA_BRANCH ** -0.5)
    inputs["diff_w_in"] = nrm((ND, D, DIFF_IN), D ** -0.5)
    inputs["diff_lambda_q1"] = nrm((ND, HEAD_DIM), 0.1)
    inputs["diff_lambda_k1"] = nrm((ND, HEAD_DIM), 0.1)
    inputs["diff_lambda_q2"] = nrm((ND, HEAD_DIM), 0.1)
    inputs["diff_lambda_k2"] = nrm((ND, HEAD_DIM), 0.1)
    inputs["diff_subln_g"] = 1.0 + nrm((ND, DIFF_V_DIM), 0.02)
    inputs["diff_w_out"] = nrm((ND, DIFF_BRANCH, D), DIFF_BRANCH ** -0.5)
    inputs["mlstm_w_in"] = nrm((NM, D, MLSTM_IN), D ** -0.5)
    inputs["mlstm_conv_w"] = nrm((NM, MLSTM_CONV_K, MLSTM_INNER), MLSTM_CONV_K ** -0.5)
    inputs["mlstm_conv_b"] = nrm((NM, MLSTM_INNER), 0.02)
    inputs["mlstm_w_q"] = nrm((NM, MLSTM_N_BLOCKS, MLSTM_QKV_BLOCK, MLSTM_QKV_BLOCK), MLSTM_QKV_BLOCK ** -0.5)
    inputs["mlstm_w_k"] = nrm((NM, MLSTM_N_BLOCKS, MLSTM_QKV_BLOCK, MLSTM_QKV_BLOCK), MLSTM_QKV_BLOCK ** -0.5)
    inputs["mlstm_w_v"] = nrm((NM, MLSTM_N_BLOCKS, MLSTM_QKV_BLOCK, MLSTM_QKV_BLOCK), MLSTM_QKV_BLOCK ** -0.5)
    inputs["mlstm_w_gate_f"] = nrm((NM, gate_in, 2 * H), 0.1 * gate_in ** -0.5)
    inputs["mlstm_b_gate_f"] = gate_bias()
    inputs["mlstm_w_gate_b"] = nrm((NM, gate_in, 2 * H), 0.1 * gate_in ** -0.5)
    inputs["mlstm_b_gate_b"] = gate_bias()
    inputs["mlstm_mh_norm_g"] = 1.0 + nrm((NM, MLSTM_INNER), 0.02)
    inputs["mlstm_skip"] = 1.0 + nrm((NM, MLSTM_INNER), 0.02)
    inputs["mlstm_w_out"] = nrm((NM, MLSTM_INNER, D), MLSTM_INNER ** -0.5)
    inputs["final_norm_g"] = 1.0 + nrm((D,), 0.02)
    return inputs

def reference(x_prompt, x_sample, cache_gqa_k, cache_gqa_v, cache_diff_k, cache_diff_v,
              state_mlstm_C, state_mlstm_n, state_mlstm_m, c, c_ctx,
              norm_g, w_mod, b_mod,
              gqa_w_in, gqa_q_norm_g, gqa_k_norm_g, gqa_w_out,
              diff_w_in, diff_lambda_q1, diff_lambda_k1, diff_lambda_q2, diff_lambda_k2, diff_subln_g, diff_w_out,
              mlstm_w_in, mlstm_conv_w, mlstm_conv_b, mlstm_w_q, mlstm_w_k, mlstm_w_v,
              mlstm_w_gate_f, mlstm_b_gate_f, mlstm_w_gate_b, mlstm_b_gate_b,
              mlstm_mh_norm_g, mlstm_skip, mlstm_w_out,
              final_norm_g):
    rows = x_sample.shape[1] // GRID_W
    cos, sin = axial_rope_tables(rows)
    xp, xs = x_prompt, x_sample
    bp = xp.shape[0]
    gqa_k_list, gqa_v_list, diff_k_list, diff_v_list = [], [], [], []
    mC_list, mn_list, mm_list = [], [], []
    for i in range(DEPTH):
        kind, j = i % N_MIXERS, i // N_MIXERS
        sh_p, sc_p, gt_p = adaln(c_ctx, w_mod[i], b_mod[i])
        sh_s, sc_s, gt_s = adaln(c, w_mod[i], b_mod[i])
        hp = rms_norm(xp, norm_g[i]) * (1.0 + sc_p) + sh_p
        hs = rms_norm(xs, norm_g[i]) * (1.0 + sc_s) + sh_s
        if kind == 0:
            op, kp, vp = gqa_context(hp, gqa_w_in[j], gqa_q_norm_g[j], gqa_k_norm_g[j], gqa_w_out[j])
            os_ = gqa_latent(hs, cache_gqa_k[:, j], cache_gqa_v[:, j], cos, sin,
                             gqa_w_in[j], gqa_q_norm_g[j], gqa_k_norm_g[j], gqa_w_out[j])
            gqa_k_list.append(kp)
            gqa_v_list.append(vp)
        elif kind == 1:
            lam_init = diff_lambda_init(i)
            lam = diff_lambda(diff_lambda_q1[j], diff_lambda_k1[j], diff_lambda_q2[j], diff_lambda_k2[j], lam_init)
            op, kp, vp = diff_context(hp, lam, lam_init, diff_w_in[j], diff_subln_g[j], diff_w_out[j])
            os_ = diff_latent(hs, cache_diff_k[:, j], cache_diff_v[:, j], cos, sin, lam, lam_init,
                              diff_w_in[j], diff_subln_g[j], diff_w_out[j])
            diff_k_list.append(kp)
            diff_v_list.append(vp)
        else:
            prm = (mlstm_w_in[j], mlstm_conv_w[j], mlstm_conv_b[j], mlstm_w_q[j], mlstm_w_k[j], mlstm_w_v[j],
                   mlstm_w_gate_f[j], mlstm_b_gate_f[j], mlstm_w_gate_b[j], mlstm_b_gate_b[j],
                   mlstm_mh_norm_g[j], mlstm_skip[j], mlstm_w_out[j])
            C0 = jnp.zeros((bp, 2, MLSTM_HEADS, MLSTM_HEAD_DIM, MLSTM_HEAD_DIM), jnp.float32)
            n0 = jnp.zeros((bp, 2, MLSTM_HEADS, MLSTM_HEAD_DIM), jnp.float32)
            m0 = jnp.zeros((bp, 2, MLSTM_HEADS), jnp.float32)
            op, Cp, np_, mp_ = mlstm_mixer(hp, C0, n0, m0, *prm)
            os_, _, _, _ = mlstm_mixer(hs, state_mlstm_C[:, j], state_mlstm_n[:, j], state_mlstm_m[:, j], *prm)
            mC_list.append(Cp)
            mn_list.append(np_)
            mm_list.append(mp_)
        xp = xp + gt_p * op
        xs = xs + gt_s * os_
    y_prompt = rms_norm(xp, final_norm_g)
    y_sample = rms_norm(xs, final_norm_g)
    new_cache_gqa_k = jnp.stack(gqa_k_list, axis=1)
    new_cache_gqa_v = jnp.stack(gqa_v_list, axis=1)
    new_cache_diff_k = jnp.stack(diff_k_list, axis=1)
    new_cache_diff_v = jnp.stack(diff_v_list, axis=1)
    new_state_mlstm_C = jnp.stack(mC_list, axis=1)
    new_state_mlstm_n = jnp.stack(mn_list, axis=1)
    new_state_mlstm_m = jnp.stack(mm_list, axis=1)
    return (y_prompt, y_sample, new_cache_gqa_k, new_cache_gqa_v, new_cache_diff_k, new_cache_diff_v,
            new_state_mlstm_C, new_state_mlstm_n, new_state_mlstm_m)


_drawn_inputs = setup_inputs


def setup_inputs(seed=0):
    import zlib

    import numpy as np

    out = dict(_drawn_inputs(seed))
    spreads = {}
    factors = {'cache_gqa_k': 8.0,
     'cache_gqa_v': 6.619,
     'state_mlstm_n': 4.892,
     'state_mlstm_m': 2.986,
     'gqa_q_norm_g': 8.0,
     'gqa_k_norm_g': 2.734,
     'diff_lambda_q1': 8.0,
     'diff_lambda_k1': 8.0,
     'diff_lambda_q2': 8.0,
     'diff_lambda_k2': 8.0,
     'diff_subln_g': 8.0,
     'mlstm_mh_norm_g': 8.0,
     'mlstm_skip': 8.0}
    for name, (base, spread) in spreads.items():
        noise = np.random.default_rng([zlib.crc32(name.encode()), seed]).standard_normal(out[name].shape)
        drawn = base * np.exp(spread * noise) if base else spread * noise
        out[name] = __import__('jax').numpy.asarray(drawn.astype(out[name].dtype))
    for name, factor in factors.items():
        out[name] = (out[name] * factor).astype(out[name].dtype)
    return out
```

```python
import math
from contextlib import ExitStack

import numpy as np
import concourse.bass as bass
from concourse import mybir

F32 = mybir.dt.float32
F32R = mybir.dt.float32r
ALU = mybir.AluOpType
ACT = mybir.ActivationFunctionType
AX = mybir.AxisListType

P = 128
D = 1024
KT = D // P
NP_, NS = 128, 512
T = NP_ + NS
PAST = 128
HD = 64
DEPTH = 4
EPS = 1e-6
SM = HD ** -0.5
AO = 192
TO = 128
QT = T // P
GQ_KV = 4
GQ_Q = 16
MI = 2048
MH = 4
MD = MI // MH
MB = MD // P
RAW, SPL = 3, 3


class Seen:

    def __init__(self):
        self.count, self.per, self.marks, self.i = {}, {}, {}, None

    def value(self, name, count):
        per = self.per.get(name, 0) if self.i is not None else 0
        return self.i * per + count if per else count

    def __call__(self, sem, by=1):
        self.count[sem.name] = self.count.get(sem.name, 0) + by
        return sem, self.value(sem.name, self.count[sem.name])

    def lend(self, buffer, sem, by=1):
        self.count[sem.name] = self.count.get(sem.name, 0) + by
        self.marks[buffer] = (sem, self.count[sem.name])

    def back(self, eng, buffer):
        if buffer in self.marks:
            sem, count = self.marks[buffer]
            eng.wait_ge(sem, self.value(sem.name, count))

    def repeat(self, eng, times, body):
        start = dict(self.count)
        body(0)
        per = {k: v - start.get(k, 0) for k, v in self.count.items()}
        if times > 1:
            self.marks = {k: (s, c - per[s.name]) for k, (s, c) in self.marks.items()}
            with eng.Fori(1, times) as i:
                self.count, self.per, self.i = {k: start.get(k, 0) for k in per}, per, i
                body(i)
            self.i = None
            again = {k: v - start.get(k, 0) for k, v in self.count.items()}
            assert all(v in (0, per[k]) for k, v in again.items())
            self.marks = {k: (s, c + (times - 1) * per[s.name]) for k, (s, c) in self.marks.items()}
        self.count = {k: start.get(k, 0) + per[k] + (times - 1) * (again[k] if times > 1 else 0) for k in per}


class Turns:

    def __init__(self):
        self.k = 0

    def __call__(self):
        self.k += 1
        return (self.k - 1) % 2


def halves():
    return ((0, AO), (320, AO + 320))


def lambda_init(layer):
    return 0.8 - 0.6 * math.exp(-0.3 * layer)


def build(nc, A, O, scratch):
    kinds = ["gqa", "diff", "mlstm", "gqa"]
    with ExitStack() as ctx:
        def sb(name, shape, dt=F32, c=None):
            return (c or ctx).enter_context(nc.sbuf_tensor(name, shape, dt))

        def sem(name):
            return ctx.enter_context(nc.semaphore(name))

        x = sb("x", [P, KT, T])
        hh = sb("hh", [P, KT, T], F32R)
        hl = sb("hl", [P, KT, T], F32R)
        raw = sb("raw", [P, RAW, KT, P])
        wh = sb("wh", [P, SPL, KT, P], F32R)
        wl = sb("wl", [P, SPL, KT, P], F32R)
        consts = sb("consts", [P, 4, P])
        ident, ones, half1, perm = (consts[:, i, :] for i in range(4))
        cols = sb("cols", [P, 3, P])
        cond = sb("cond", [P, 2 * KT])
        mod = sb("mod", [P, 24, 2])
        amul = sb("amul", [P, KT, 2])
        rinv = sb("rinv", [P, T])
        two = sb("two", [P, 2, T])
        ht = sb("ht", [P, 2, T])
        eps = sb("eps", [P, 1])
        idle = sb("idle", [P, 1])
        cs = sb("cs", [P, 2, NS])

        NORMG = 96
        FING, QG, KG, SUBG, LAM = 16, 24, 26, 28, 29
        CONVB, CONVW, MHG, SKIP = 0, 16, 80, 96

        att = ExitStack()
        yh = sb("yh", [P, KT, T], F32R, att)
        yl = sb("yl", [P, KT, T], F32R, att)
        z = sb("z", [P, 2, T], F32, att)
        kv = sb("kv", [P, T + PAST], F32, att)
        qn = sb("qn", [P, 2, T], F32, att)
        kst = sb("kst", [P, 2, 2, T + PAST], F32R, att)
        qst = sb("qst", [P, 4, T], F32R, att)
        vtm = sb("vtm", [P, QT + 1, P], F32, att)
        ck = sb("ck", [P, P], F32, att)
        kp = sb("kp", [P, P], F32, att)
        comb = sb("comb", [P, T], F32, att)
        osb = sb("osb", [P, QT, P], F32, att)
        st = sb("st", [P, 4, 8], F32, att)
        lamr = sb("lamr", [P, 4, HD], F32, att)
        lamt = sb("lamt", [P, 8], F32, att)
        oss = sb("oss", [P, 8], F32, att)
        att.close()

        AW = 11 * P
        ml = ExitStack()
        xm = sb("xm", [P, MB, T + 5], F32, ml)
        xc = sb("xc", [P, MB, T], F32, ml)
        wsm = sb("wsm", [P, 3, MI // P, 4], F32, ml)
        bd = sb("bd", [P, 3, MB, P], F32, ml)
        gbias = sb("gbias", [P, 16], F32, ml)
        mc = sb("mc", [P, 4 * P], F32, ml)
        place, headmask = mc[0:16, 0:P], mc[:, P:2 * P]
        m0 = sb("m0", [64, 1], F32, ml)
        nml = sb("nml", [64, 1], F32, ml)
        mnew = sb("mnew", [64, 1], F32, ml)
        mrow = sb("mrow", [64, T], F32, ml)
        emrow = sb("emrow", [64, T], F32, ml)
        wirow = sb("wirow", [64, T], F32, ml)
        ct = sb("ct", [P, 6, 64], F32, ml)
        ccol = sb("ccol", [P, 2, 6], F32, ml)
        sel = sb("sel", [64, 2, P], F32, ml)
        hcol = sb("hcol", [P, 24], F32, ml)
        nall = sb("nall", [P, 2, MI // P], F32, ml)
        idle3 = sb("idle3", [P, 1], F32, ml)
        first = ExitStack()
        crow = sb("crow", [64, T], F32, first)
        rones = sb("rones", [64, T], F32, first)
        wg = sb("wg", [P, 3 * MI // P, 16], F32, first)
        bdt = sb("bdt", [P, 12, P], F32, first)
        gm = sb("gm", [P, MB, 32], F32, first)
        cv = sb("cv", [P, 2, T + 5], F32, first)
        nrow = sb("nrow", [2 * MI // P, P], F32, first)
        g16 = sb("g16", [16, T], F32, first)
        r1 = sb("r1", [64, T], F32, first)
        r2 = sb("r2", [64, T], F32, first)
        first.close()
        second = ExitStack()
        mq = sb("mq", [P, MB, T], F32, second)
        mk = sb("mk", [P, MB, T], F32, second)
        mv = sb("mv", [P, QT, MD], F32, second)
        ktm = sb("ktm", [P, MD], F32, second)
        amat = sb("amat", [P, 2 * AW], F32, second)
        mdg = sb("mdg", [P, 2, T], F32, second)
        nrep = sb("nrep", [P, MB, P], F32, second)
        second.close()
        ml.close()
        def cst(u):
            return amat[:, u * 1024:(u + 1) * 1024].rearrange("p (a c) -> p a c", a=2)

        def nst(d):
            return mdg[0:1, d, 0:MD]

        back = ExitStack()
        sb("under_yh_yl", [P, 2, KT, T], F32, back)
        yb = sb("yb", [P, 2, KT, T], F32, back)
        back.close()

        acc = [ctx.enter_context(nc.psum_tensor(f"acc{b}", [P, 1024], F32)) for b in range(2)]
        pt = ctx.enter_context(nc.psum_tensor("pt", [P, 1024], F32))
        ob = [ctx.enter_context(nc.psum_tensor(f"ob{b}", [P, 512], F32)) for b in range(2)]

        raw_full = [sem(f"raw_full{s}") for s in range(RAW)]
        raw_used = [sem(f"raw_used{s}") for s in range(RAW)]
        w_full = [sem(f"w_full{s}") for s in range(SPL)]
        proj_done = [sem(f"proj_done{s}") for s in range(SPL)]
        acc_full = [sem(f"acc_full{b}") for b in range(2)]
        acc_free = [sem(f"acc_free{b}") for b in range(2)]
        ob_full = [sem(f"ob_full{b}") for b in range(2)]
        ob_free = [sem(f"ob_free{b}") for b in range(2)]
        xin_full = [sem(f"xin_full{b}") for b in range(2)]
        y_stored = [sem(f"y_stored{b}") for b in range(2)]
        names = """const_in rows_in eps_set cols_turned cols_ready cond_ready x_in x_ready lam_sum lam_exp lam_ready
            lam_sent pool_step act_step dve_step sq_full sq_used root_ready mod_ready xr_full xr_used ht_full h_ready
            nroot_ready qk_scaled rot_read qk_turned hi_ready st_ready raw_copied cache_full vc_full v_used
            nb_ready p_ready e_ready comb_ready pts_dve pts_act pt_full osb_ready oroot_ready o_scaled yt_ready yhi_ready y_ready
            tm_ready store_k store_v normed out_ready""".split()
        (const_in, rows_in, eps_set, cols_turned, cols_ready, cond_ready, x_in, x_ready, lam_sum, lam_exp,
         lam_ready, lam_sent, pool_step, act_step, dve_step, sq_full, sq_used, root_ready, mod_ready, xr_full, xr_used,
         ht_full, h_ready, nroot_ready, qk_scaled, rot_read, qk_turned, hi_ready, st_ready, raw_copied, cache_full,
         vc_full, v_used, nb_ready, p_ready, e_ready, comb_ready, pts_dve, pts_act, pt_full, osb_ready, oroot_ready,
         o_scaled, yt_ready, yhi_ready, y_ready, tm_ready, store_k, store_v, normed, out_ready) = map(sem, names)

        names = """m_begin m_end m_in m_zeroed m_ones bd_ready bt_ready gm_ready xm_copied xc_done cv_ready gates_done
            spill g_full g_copied row_read ln_ready mact_step m_made rows_ready xmc_full qkv_copied mb_full mdiag_ready
            d_full a_made eb_full eb_read wb_full wb_read qw_full h_done h_sum centred kw_ready cst_copied n_full
            n_copied n_stored msq_full msq_used mroot_ready ym_ready y_spill m_stored""".split()
        (m_begin, m_end, m_in, m_zeroed, m_ones, bd_ready, bt_ready, gm_ready, xm_copied, xc_done, cv_ready, gates_done,
         spill, g_full, g_copied, row_read, ln_ready, mact_step, m_made, rows_ready, xmc_full, qkv_copied, mb_full, mdiag_ready,
         d_full, a_made, eb_full, eb_read, wb_full, wb_read, qw_full, h_done, h_sum, centred, kw_ready, cst_copied, n_full,
         n_copied, n_stored, msq_full, msq_used, mroot_ready, ym_ready, y_spill, m_stored) = map(sem, names)
        c_full = [sem(f"c_full{b}") for b in range(2)]
        c_used = [sem(f"c_used{b}") for b in range(2)]
        c_stored = [sem(f"c_stored{b}") for b in range(2)]
        yb_full = [sem(f"yb_full{b}") for b in range(2)]

        rows = rinv[:, 0:3 * P].rearrange("p (a c) -> p a c", a=3)
        xtile = [two[:, :, 0:512], ht[:, :, 0:512]]
        NLAM, SUBS = 5, 6
        L1 = lambda_init(1)
        BM = P * 3

        def w_at(w, c, n=P):
            return w.rearrange("(kt p) c -> p kt c", p=P)[:, :, bass.ds(c, n)]

        XR = [2 * KT if kind == "mlstm" else KT for kind in kinds]
        PANELS = {"gqa": (12, 12, 4), "diff": (20, 20, 0)}
        steps = [(qt, j) for qt in range(QT) for j in range(2)]
        NST = len(steps)

        def head_cols(h, n):
            return slice(h * MB + n, h * MB + n + 1) if isinstance(h, int) else bass.ds(h * MB + n, 1)

        def xm_at(blk, c0, c1):
            o = 2 if c1 <= P else 4
            return xm[:, blk, c0 + o:c1 + o]

        GROUPS = ((P, T, 0), (0, P, 512))

        def tri(d, i):
            if i == 0:
                return 0, P, 0
            s = i - 1
            before = sum((4 - u) if d == 0 else (u + 1) for u in range(s))
            return ((P + s * P, T) if d == 0 else (P, P + (s + 1) * P)) + ((1 + before) * P,)

        def mlstm_sp(sp, seen, whole):
            w = A["mlstm_w_in"][0]
            sp.wait_ge(m_begin, 1)
            for i, name in enumerate(("mlstm_w_q", "mlstm_w_k", "mlstm_w_v")):
                sp.dma_start(wsm[:, i, :, :], A[name][0].rearrange("(b n) c d -> (n c) b d", n=32)).then_inc(m_in, 16)
            for g, name in enumerate("fb"):
                sp.dma_start(wg[:, :, g * 8:(g + 1) * 8], A[f"mlstm_w_gate_{name}"][0].rearrange("(b p) c -> p b c", p=P)).then_inc(m_in, 16)
                sp.dma_start(gbias[0:1, g * 8:(g + 1) * 8], A[f"mlstm_b_gate_{name}"]).then_inc(m_in, 16)
            sp.dma_start(mc[:, :], A["consts"][:, 4 * P + 2 * NS:]).then_inc(m_in, 16)
            sp.dma_start(nrow[:, :], A["state_mlstm_n"][0, 0].rearrange("d h (k p) -> (d h k) p", p=P)).then_inc(m_in, 16)
            sp.wait_ge(m_zeroed, 1)
            for d in range(2):
                sp.dma_start(m0[32 * d:32 * d + MH, :], A["state_mlstm_m"][0, 0, d].rearrange("(h a) -> h a", a=1)).then_inc(m_in, 16)

            def head_a(h):
                for blk in range(MB):
                    whole(blk % 2, w, h * (MB * P) + blk * P)
            seen.repeat(sp, MH, head_a)
            seen.back(sp, ("raw", 2))

            def head_b(h):
                seen.back(sp, "xmc")
                if seen.i is None:
                    sp.wait_ge(spill, 32 * MH)
                    sp.wait_ge(gates_done, MH)
                sp.dma_start(xm[:, :, :], scratch["xm"][bass.ds(h, 1)].rearrange("a b p t -> p (a b) t")).then_inc(xmc_full, 16)
                sp.dma_start(xc[:, :, :], scratch["xc"][bass.ds(h, 1)].rearrange("a b p t -> p (a b) t")).then_inc(xmc_full, 16)
                seen.lend("xmc", ym_ready)
                for blk in range(MB):
                    whole(blk % 2, w, h * (MB * P) + blk * P + MI)
                cd = A["state_mlstm_C"][0, 0].rearrange("d h (k p) e -> d p h k e", p=P)
                for d in range(2):
                    for kt in range(4):
                        s = kt % 2
                        seen.back(sp, ("c", s))
                        sp.dma_start(raw[:, 2, 4 * s:4 * s + 4, :],
                                     cd[d][:, bass.ds(h, 1), kt, :].rearrange("p a (b e) -> p (a b) e", b=4)).then_inc(c_full[s], 16)
                        seen.lend(("c", s), c_used[s])
            seen.repeat(sp, MH, head_b)
            sp.wait_ge(y_spill, 16 * MH)
            sp.wait_ge(m_end, 1)
            for r in range(2):
                sp.dma_start(yb[:, r, :, :], scratch["y"][8 * r:8 * r + 8].rearrange("b p t -> p b t")).then_inc(yb_full[r], 16)
            wo = A["mlstm_w_out"][0]
            for r in range(2):
                def outs(i, r=r):
                    for s in range(2):
                        whole(s, wo[r * D:(r + 1) * D, :], i * (2 * P) + s * P)
                seen.repeat(sp, KT // 2, outs)

        def mlstm_pool(pool, seen, split):
            pool.wait_ge(m_begin, 1)
            pool.memset(m0[:, :], 0.0).then_inc(m_zeroed, 1)

            def four(i):
                for s in (0, 1, 0, 1):
                    split(s)
            seen.repeat(pool, 2 * MH, four)
            seen.repeat(pool, 4, four)

        def mlstm_pe(pe, seen, turn, buffer, project):
            def pair(dst, lhsT, src, start, stop):
                for c0, c1, o in GROUPS:
                    ins = pe.matmul(dst(o, c1 - c0), lhsT, src(c0, c1), start=start, stop=stop, skip_group_check=True)
                return ins

            pe.wait_ge(m_in, 16 * 11)

            def head_a(h):
                pe.wait_ge(*seen(bd_ready))
                b = buffer(bt_ready)
                for n in range(8):
                    ins = pe.transpose(acc[b][:, n * P:(n + 1) * P], bd[:, n // 4, n % 4, :], ident)
                ins.then_inc(acc_full[b], 1)
                b = buffer(bt_ready)
                for n in range(4):
                    ins = pe.transpose(acc[b][:, n * P:(n + 1) * P], bd[:, 2, n, :], ident)
                ins.then_inc(acc_full[b], 1)
                seen.marks["bt"] = seen.marks[("acc", b)]
                project(0, ready=h_ready if seen.i is None else None, freed_by=xm_copied)
                b = buffer(gm_ready)
                seen.marks["gm"] = seen.marks[("acc", b)]
                seen.back(pe, "bt")
                for blk in range(MB):
                    for n in range(3):
                        ins = pe.matmul(acc[b][:, blk * 32 + 16 * (n // 2):blk * 32 + 16 * (n // 2) + 16], bdt[:, n * 4 + blk, :],
                                        wg[:, head_cols(h, n * 16 + blk), :].rearrange("p a c -> p (a c)"),
                                        start=n != 1, stop=n != 0, skip_group_check=True)
                ins.then_inc(acc_full[b], 1)
                for s in (1, 0, 1):
                    project(s, freed_by=xm_copied)
                turn()
                seen.back(pe, "gm")
                pe.wait_ge(*seen(xc_done, MB))
                for blk in range(MB):
                    first = seen.i is None and blk == 0
                    pair(lambda o, w: pt[0:16, o:o + w], gm[:, blk, 0:16], lambda c0, c1: xc[:, blk, c0:c1], first, False)
                    ins = pair(lambda o, w: pt[0:16, o:o + w], gm[:, blk, 16:32], lambda c0, c1: xm_at(blk, c0, c1), False, False)
                ins.then_inc(gates_done, 1)
            seen.repeat(pe, MH, head_a)

            pe.wait_ge(*seen(m_ones))
            pair(lambda o, w: pt[0:16, o:o + w], gbias[0:1, :], lambda c0, c1: rones[0:1, c0:c1], False, True).then_inc(g_full, 1)
            seen.lend("pt", g_copied)
            seen.back(pe, "pt")
            for n in range(2):
                b = buffer(row_read)
                pair(lambda o, w: acc[b][0:64, o:o + w], place[:, n * 64:n * 64 + 64], lambda c0, c1: g16[0:16, c0:c1], True, True)\
                    .then_inc(acc_full[b], 1)
            b = buffer(row_read)
            pe.wait_ge(*seen(rows_ready))
            for n in range(6):
                src = crow[:, n * P:(n + 1) * P] if n < 5 else wirow[:, 0:P]
                pe.transpose(acc[b][:, n * 64:(n + 1) * 64], src, ident[0:64, 0:64])
            ins = pe.transpose(acc[b][:, 384:416], nrow[:, :], ident[0:32, 0:32])
            ins.then_inc(acc_full[b], 1)

            def rows_to(dst, src, d, n):
                return pair(dst, sel[:, d, :], src, True, True)

            def head_b(h):
                pe.wait_ge(*seen(bd_ready))
                pe.wait_ge(*seen(xmc_full, 32))
                for n in range(2):
                    for blk in range(MB):
                        b = buffer(qkv_copied)
                        for t, c in halves():
                            ins = pe.matmul(acc[b][:, c:c + 320], bd[:, n, blk, :], xc[:, blk, t:t + 320], start=True, stop=True)
                        ins.then_inc(acc_full[b], 1)
                for tiles in ((0, 1), (2, 3), (4, 5)):
                    b = buffer(qkv_copied)
                    for u, t in enumerate(tiles):
                        for blk in range(MB):
                            lhsT = xc[:, blk, 0:P] if t == 5 else xm_at(blk, t * P, (t + 1) * P)
                            ins = pe.matmul(acc[b][:, u * 512 + blk * P:u * 512 + (blk + 1) * P], lhsT,
                                            bd[:, 1 if t == 5 else 2, blk, :], start=True, stop=True)
                    ins.then_inc(acc_full[b], 1)
                seen.marks["qkv"] = seen.marks[("acc", b)]
                for d in range(2):
                    for buf in (("pt",), ("ob0", "ob1"))[d]:
                        seen.back(pe, buf)
                    dst = (lambda o, w: pt[:, o:o + w]) if d == 0 else (lambda o, w: ob[o // 512][:, 0:w])
                    rows_to(dst, lambda c0, c1: mrow[:, c0:c1], d, h).then_inc(mb_full, 1)
                seen.lend("pt", d_full, 10)
                seen.marks["ob0"] = seen.marks["ob1"] = seen.marks["pt"]
                seen.back(pe, "qkv")
                for i in range(QT):
                    b = buffer(None)
                    seen.lend(("acc", b), a_made, 2)
                    seen.marks["a"] = seen.marks[("acc", b)]
                    r = (0, P) if i == 0 else (P, T)
                    for kt in range(4):
                        ins = pe.matmul(acc[b][:, 0:r[1] - r[0]], mk[:, kt, i * P:(i + 1) * P], mq[:, kt, r[0]:r[1]],
                                        start=kt == 0, stop=kt == 3)
                    ins.then_inc(acc_full[b], 1)
                for s in (0, 1, 0, 1):
                    project(s)
                for d in range(2):
                    for buf in ("ob0", "ob1", "pt"):
                        seen.back(pe, buf)
                    rows_to(lambda o, w: ob[o // 512][:, 0:w], lambda c0, c1: emrow[:, c0:c1], d, h).then_inc(eb_full, 1)
                    pe.matmul(pt[:, 0:512], sel[:, d, :], wirow[:, P:T], start=True, stop=True).then_inc(wb_full, 1)
                    seen.lend("ob0", eb_read)
                    seen.lend("pt", wb_read)
                    if d == 0:
                        seen.back(pe, "a")
                    seen.back(pe, "ob0")
                    seen.back(pe, "pt")
                    bb = [buffer(None), buffer(None)]
                    seen.lend("num", h_done)
                    for buf in (("acc", 0), ("acc", 1), "ob0", "ob1", "pt"):
                        seen.marks[buf] = seen.marks["num"]
                    num = lambda e: acc[bb[e // 2]][:, (e % 2) * 512:(e % 2) * 512 + 512]
                    for e in range(4):
                        pe.matmul(pt[:, 512 + e * P:512 + (e + 1) * P], mv[:, 0, e * P:(e + 1) * P], amat[:, d * AW:d * AW + P],
                                  start=True, stop=True, skip_group_check=True)
                    pe.matmul(ob[1][:, 0:P], ones, amat[:, d * AW:d * AW + P], start=True, stop=True)
                    order = range(1, 5) if d == 0 else range(4, 0, -1)
                    for n, i in enumerate(order):
                        c0, c1, o = tri(d, i)
                        a = amat[:, d * AW + o:d * AW + o + c1 - c0]
                        for e in range(4):
                            pe.matmul(num(e)[:, c0 - P:c1 - P], mv[:, i, e * P:(e + 1) * P], a, start=n == 0, stop=False,
                                      skip_group_check=True)
                        pe.matmul(ob[0][:, c0 - P:c1 - P], ones, a, start=n == 0, stop=False, skip_group_check=True)
                    for kt in range(4):
                        s = kt % 2
                        pe.wait_ge(*seen(qw_full))
                        pe.wait_ge(*seen(c_full[s], 16))
                        for e in range(4):
                            pe.matmul(num(e), raw[:, 2, 4 * s + e, :], mdg[:, s, 0:NS], start=False, stop=kt == 3, skip_group_check=True)
                        ins = pe.matmul(ob[0][:, :], nrep[:, kt, :], mdg[:, s, 0:NS], start=False, stop=kt == 3,
                                        skip_group_check=True)
                        ins.then_inc(c_used[s], 1)
                pe.wait_ge(*seen(h_sum))
                b = buffer(centred)
                for blk in range(MB):
                    for t, c in halves():
                        ins = pe.matmul(acc[b][:, c:c + 320], ones, xm[:, blk, t:t + 320], start=blk == 0, stop=blk == 3)
                ins.then_inc(acc_full[b], 1)
                seen.back(pe, "ob0")
                seen.back(pe, "ob1")
                for d in range(2):
                    pe.wait_ge(*seen(kw_ready))
                    for u in range(2):
                        b = buffer(cst_copied)
                        for v in range(2):
                            kb = 2 * u + v
                            ins = pe.matmul(acc[b][:, v * 512:v * 512 + 512], two[:, d, kb * P:(kb + 1) * P], mv[:, 0, :], start=True, stop=True)
                        ins.then_inc(acc_full[b], 1)
                    ins = pe.matmul(ob[d][0:1, :], ones[:, 0:1], two[:, d, 0:MD], start=True, stop=True)
                ins.then_inc(n_full, 1)
                seen.lend("ob0", n_copied)
                seen.marks["ob1"] = seen.marks["ob0"]
                b = buffer(mroot_ready)
                for blk in range(MB):
                    pe.wait_ge(*seen(msq_full))
                    for t, c in halves():
                        ins = pe.matmul(acc[b][:, c:c + 320], ones, ht[:, blk % 2, t:t + 320], start=blk == 0, stop=blk == 3)
                    ins.then_inc(msq_used if blk < 3 else acc_full[b], 1)
            seen.repeat(pe, MH, head_b)

            for r in range(2):
                pe.wait_ge(*seen(y_ready, KT))
                def outs(i, r=r):
                    for s in range(2):
                        project(s, *((hh, hl) if r == 0 else (yh, yl)), freed_by=x_ready)
                seen.repeat(pe, KT // 2, outs)
            for s in range(2):
                seen(raw_full[s], 32 * (4 * MH + KT))

        def mlstm_act(act, seen, turn, use):
            seen.back(act, "vtm0")
            seen.back(act, "kp")
            act.copy(idle3[:, :], eps[:, :]).then_inc(m_begin, 1)

            def head_a(h):
                use(), use()
                seen.back(act, "xmc")
                seen.back(act, "spill")

                def silu(blk):
                    act.wait_ge(*seen(cv_ready))
                    act.activation(xc[:, blk, 0:P], cv[:, blk % 2, 0:P], ACT.Silu, bias=hcol[:, blk:blk + 1])
                    act.activation(xc[:, blk, P:T], cv[:, blk % 2, P + 2:T + 2], ACT.Silu, bias=hcol[:, blk:blk + 1]).then_inc(xc_done, 1)

                for blk in range(MB):
                    b, _ = use(False)
                    act.wait_ge(*seen(proj_done[blk % 2]))
                    act.copy(xm_at(blk, 0, P), acc[b][:, AO:AO + P])
                    act.copy(xm_at(blk, P, T), acc[b][:, AO + P:AO + T]).then_inc(xm_copied, 1)
                    if blk == 0:
                        use()
                    if blk:
                        silu(blk - 1)
                turn()
                silu(MB - 1)
                act.wait_ge(*seen(xc_done, MB))
                seen(xm_copied, MB)
                act.dma_start(scratch["xm"][bass.ds(h, 1)].rearrange("a b p t -> p (a b) t"), xm[:, :, :]).then_inc(spill, 16)
                act.dma_start(scratch["xc"][bass.ds(h, 1)].rearrange("a b p t -> p (a b) t"), xc[:, :, :]).then_inc(spill, 16)
                seen.lend("spill", spill, 32)
                seen.lend("xmc", gates_done)
            seen.repeat(act, MH, head_a)

            act.wait_ge(*seen(g_full))
            for c0, c1, o in GROUPS:
                ins = act.copy(g16[0:16, c0:c1], pt[0:16, o:o + c1 - c0])
            ins.then_inc(g_copied, 1)
            use()
            b, full = use()
            act.wait_ge(*full)
            for c0, c1, o in GROUPS:
                ins = act.activation(r1[:, c0:c1], acc[b][0:64, o:o + c1 - c0], ACT.Abs)
            ins.then_inc(mact_step, 1)
            act.wait_ge(*seen(mact_step))
            act.activation(r1[:, :], r1[:, :], ACT.Exp, scale=-1.0).then_inc(mact_step, 1)
            act.wait_ge(*seen(mact_step))
            act.activation(r1[:, :], r1[:, :], ACT.Ln, bias=ones[0:64, 0:1]).then_inc(ln_ready, 1)
            act.wait_ge(*seen(m_made))
            act.activation(emrow[:, :], emrow[:, :], ACT.Exp, scale=-1.0)
            act.activation(wirow[:, P:T], mrow[:, P:T], ACT.Exp, scale=-1.0, bias=m0[:, 0:1])
            act.activation(wirow[:, 0:P], crow[:, 0:P], ACT.Exp, bias=nml[:, 0:1]).then_inc(rows_ready, 1)
            use()

            def head_b(h):
                for n in range(2):
                    for blk in range(MB):
                        b, full = use()
                        act.wait_ge(*full)
                        if n == 1 and blk == 0:
                            seen.back(act, "y")
                        act.copy((mq, mk)[n][:, blk, :], acc[b][:, AO:AO + T]).then_inc(qkv_copied, 1)
                for u in range(3):
                    b, full = use()
                    act.wait_ge(*full)
                    if u < 2:
                        act.copy(mv[:, 2 * u:2 * u + 2, :], acc[b][:, :].rearrange("p (a c) -> p a c", a=2)).then_inc(qkv_copied, 1)
                    else:
                        act.copy(mv[:, 4, :], acc[b][:, 0:512])
                        act.copy(ktm[:, :], acc[b][:, 512:1024]).then_inc(qkv_copied, 1)
                act.wait_ge(*seen(mdiag_ready, 2))
                for i in range(QT):
                    use()
                    for d in range(2):
                        c0, c1, _ = tri(d, i)
                        t0 = i * P
                        if i:
                            act.wait_ge(*seen(a_made))
                        bias = ccol[:, d, i:i + 1]
                        ins = act.activation(two[:, d, t0:t0 + P], mdg[:, d, t0:t0 + P], ACT.Exp, scale=-1.0, bias=bias)
                        o0, o1 = (t0 + P, c1) if d == 0 else (c0, t0)
                        if i and o1 > o0:
                            src = pt[:, o0 - P:o1 - P] if d == 0 else ob[0][:, o0 - P:o1 - P]
                            ins = act.activation(two[:, d, o0:o1], src, ACT.Exp, scale=-1.0, bias=bias)
                        ins.then_inc(d_full, 1)
                seen(a_made, 2)
                for blk in range(MB):
                    b, _ = use(False)
                    act.wait_ge(*seen(proj_done[blk % 2]))
                    act.activation(mk[:, blk, :], acc[b][:, AO:AO + T], ACT.Silu).then_inc(acc_free[b], 1)
                for d in range(2):
                    act.wait_ge(*seen(eb_full))
                    act.copy(ht[:, 0, P:T], ob[0][:, :])
                    act.copy(ht[:, 0, 0:P], ob[1][:, 0:P]).then_inc(eb_read, 1)
                    act.wait_ge(*seen(wb_full))
                    act.copy(ht[:, 1, 0:NS], pt[:, 0:NS]).then_inc(wb_read, 1)
                    use(False), use(False)
                use()
                act.wait_ge(*seen(centred))
                for d in range(2):
                    for u in range(2):
                        b, full = use()
                        act.wait_ge(*full)
                        seen.back(act, ("cst", u))
                        act.copy(cst(u), acc[b][:, :].rearrange("p (a c) -> p a c", a=2)).then_inc(cst_copied, 1)
                        act.wait_ge(*seen(cst_copied))
                        act.dma_start(O["mlstm_C"][0, 0, d].rearrange("h (k p) e -> p h k e", p=P)[:, bass.ds(h, 1), 2 * u:2 * u + 2, :]
                                      .rearrange("p a k e -> p (a k) e"), cst(u)).then_inc(c_stored[u], 16)
                        seen.lend(("cst", u), c_stored[u], 16)
                act.wait_ge(*seen(n_full))
                seen.back(act, "nst")
                act.copy(nst(0), ob[0][0:1, :])
                act.copy(nst(1), ob[1][0:1, :]).then_inc(n_copied, 1)
                act.wait_ge(*seen(n_copied))
                for d in range(2):
                    act.dma_start(O["mlstm_n"][0, 0, d][bass.ds(h, 1), :], nst(d)).then_inc(n_stored, 16)
                seen.lend("nst", n_stored, 32)
                for blk in range(MB):
                    if blk >= 2:
                        act.wait_ge(*seen(msq_used))
                    act.activation(ht[:, blk % 2, :], xm[:, blk, 0:T], ACT.Square).then_inc(msq_full, 1)
                seen(msq_used)
                for blk in range(MB):
                    ins = act.activation(xc[:, blk, :], xc[:, blk, :], ACT.Copy, scale=hcol[:, 4 + blk:5 + blk])
                b, full = use()
                act.wait_ge(*full)
                act.activation(rinv[:, :], acc[b][:, AO:AO + T], ACT.Sqrt, bias=eps[:, :], scale=1.0 / MD).then_inc(mroot_ready, 1)
                act.wait_ge(*seen(ym_ready))
                act.dma_start(scratch["y"].rearrange("(h b) p t -> p h b t", b=MB)[:, bass.ds(h, 1), :, :].rearrange("p a b t -> p (a b) t"),
                              mk[:, :, :]).then_inc(y_spill, 16)
                seen.lend("y", y_spill, 16)
            seen.repeat(act, MH, head_b)
            for u in range(2):
                seen.back(act, ("cst", u))
            seen.back(act, "nst")
            for d in range(2):
                col = P - 1 if d == 0 else 0
                act.dma_start(O["mlstm_m"][0, 0, d].rearrange("(h a) -> h a", a=1), mnew[32 * d:32 * d + MH, 0:1]).then_inc(m_stored, 16)
            act.wait_ge(m_stored, 32)
            act.copy(idle3[:, :], eps[:, :]).then_inc(m_end, 1)
            for r in range(2):
                act.wait_ge(yb_full[r], 16)
                for kt in range(KT):
                    act.copy((hh, yh)[r][:, kt, :], yb[:, r, kt, :]).then_inc(yhi_ready, 1)
            seen(proj_done[0], KT)
            seen(proj_done[1], KT)

        def mlstm_dve(dve, seen, turn, use, step, add_gated):
            def bds(h, n3=3):
                for n in range(3):
                    for blk in range(MB):
                        ins = dve.tensor_tensor(bd[:, n, blk, :].rearrange("p (a c) -> p a c", c=4), headmask.rearrange("p (a c) -> p a c", c=4),
                                                wsm[:, n, head_cols(h, blk), :].to_broadcast([P, 32, 4]), ALU.mult)
                ins.then_inc(bd_ready, 1)

            dve.wait_ge(m_in, 16 * 11)
            for a0, a1 in ((0, 2), (P + 2, P + 4), (T + 4, T + 5)):
                dve.memset(xm[:, :, a0:a1], 0.0)
            dve.memset(rones[:, :], 1.0).then_inc(m_ones, 1)
            dve.wait_ge(*seen(m_ones))

            def head_a(h):
                for n in range(MB):
                    ins = dve.tensor_copy(hcol[:, n:n + 1], cols[:, 2, head_cols(h, CONVB + n)])
                    for k in range(4):
                        ins = dve.tensor_copy(hcol[:, 4 + 4 * k + n:5 + 4 * k + n], cols[:, 2, head_cols(h, CONVW + 16 * k + n)])
                step(ins)
                bds(h)
                for n, w in ((0, 8), (8, 4)):
                    b, full = use()
                    dve.wait_ge(*full)
                    dve.tensor_copy(bdt[:, n:n + w, :], acc[b][:, 0:w * P].rearrange("p (a c) -> p a c", c=P)).then_inc(bt_ready, 1)
                for blk in range(MB):
                    use(False)
                    dve.wait_ge(*seen(xm_copied))
                    if blk == 0:
                        b, full = use()
                        dve.wait_ge(*full)
                        dve.tensor_copy(gm[:, :, :], acc[b][:, 0:128].rearrange("p (a c) -> p a c", c=32)).then_inc(gm_ready, 1)
                    seen.back(dve, ("cv", blk % 2))
                    W = T + 2
                    step(dve.tensor_scalar(cv[:, blk % 2, 0:W], xm[:, blk, 0:W], hcol[:, 4 + blk:5 + blk], None, ALU.mult))
                    for k in range(1, 4):
                        ins = dve.scalar_tensor_tensor(out=cv[:, blk % 2, 0:W], in0=xm[:, blk, k:k + W],
                                                       scalar=hcol[:, 4 + 4 * k + blk:5 + 4 * k + blk], in1=cv[:, blk % 2, 0:W],
                                                       op0=ALU.mult, op1=ALU.add)
                        if k < 3:
                            step(ins)
                    ins.then_inc(cv_ready, 1)
                    seen.lend(("cv", blk % 2), xc_done)
                turn()
                dve.wait_ge(*seen(cv_ready, MB))
                seen.back(dve, ("cv", 1))
            seen.repeat(dve, MH, head_a)

            b, full = use()
            dve.wait_ge(*full)
            for c0, c1, o in GROUPS:
                ins = dve.tensor_copy(crow[:, c0:c1], acc[b][0:64, o:o + c1 - c0])
            ins.then_inc(row_read, 1)
            b, full = use()
            dve.wait_ge(*seen(ln_ready))
            for c0, c1, o in GROUPS:
                ins = dve.scalar_tensor_tensor(out=r2[:, c0:c1], in0=acc[b][0:64, o:o + c1 - c0], scalar=0.0, in1=r1[:, c0:c1],
                                               op0=ALU.min, op1=ALU.subtract)
            ins.then_inc(row_read, 1)
            dve.wait_ge(*seen(row_read, 2))
            segs = [(0, slice(0, P), slice(0, P)), (0, slice(P, T), slice(P, T)),
                    (32, slice(0, P), slice(P - 1, None, -1)), (32, slice(P, T), slice(T - 1, P - 1, -1))]
            for p0, _, c in segs:
                ins = dve.tensor_tensor_scan(out=emrow[p0:p0 + 32, c], data0=rones[p0:p0 + 32, c], data1=r2[p0:p0 + 32, c],
                                             initial=0.0, op0=ALU.mult, op1=ALU.add)
            step(ins)
            step(dve.tensor_tensor(crow[:, :], crow[:, :], emrow[:, :], ALU.subtract))
            for p0, f, c in segs:
                ins = dve.tensor_tensor_scan(out=mrow[p0:p0 + 32, c], data0=crow[p0:p0 + 32, c], data1=crow[p0:p0 + 32, c],
                                             initial=0.0 if f.start == 0 else m0[p0:p0 + 32, 0:1], op0=ALU.max, op1=ALU.max)
            step(ins)
            for d, col in ((0, P - 1), (1, 0)):
                ins = dve.tensor_scalar(nml[32 * d:32 * d + 32, :], mrow[32 * d:32 * d + 32, col:col + 1], -1.0, None, ALU.mult)
            step(dve.tensor_tensor(emrow[:, :], emrow[:, :], mrow[:, :], ALU.add))
            for d, col in ((0, P - 1), (1, 0)):
                ins = dve.tensor_copy(mnew[32 * d:32 * d + 32, :], emrow[32 * d:32 * d + 32, col:col + 1])
            ins.then_inc(m_made, 1)
            b, full = use()
            dve.wait_ge(*full)
            dve.tensor_copy(nall[:, :, :], acc[b][:, 384:416].rearrange("p (d c) -> p d c", d=2))
            dve.tensor_copy(ct[:, :, :], acc[b][:, 0:384].rearrange("p (a c) -> p a c", c=64)).then_inc(row_read, 1)
            dve.wait_ge(*seen(row_read))

            def head_b(h):
                for d in range(2):
                    row = slice(h + 32 * d, h + 32 * d + 1) if isinstance(h, int) else bass.ds(h + 32 * d, 1)
                    dve.tensor_copy(sel[:, d, :], ident[0:64, row].to_broadcast([64, P]))
                    dve.tensor_copy(ccol[:, d, :], ct[:, :, row].rearrange("p a b -> p (a b)"))
                for n in range(MB):
                    dve.tensor_copy(hcol[:, n:n + 1], cols[:, 2, head_cols(h, MHG + n)])
                    ins = dve.tensor_copy(hcol[:, 4 + n:5 + n], cols[:, 2, head_cols(h, SKIP + n)])
                step(ins)
                bds(h)
                for _ in range(11):
                    use()
                dve.wait_ge(*seen(mb_full, 2))
                for d in range(2):
                    mask = mc[:, (2 + d) * P:(3 + d) * P]
                    src = (pt[:, 0:512], pt[:, 512:640]) if d == 0 else (ob[0][:, :], ob[1][:, 0:P])
                    for u in range(4):
                        dve.tensor_tensor(mdg[:, d, P + u * P:P + (u + 1) * P], src[0][:, u * P:(u + 1) * P], mask, ALU.add)
                    dve.tensor_tensor(mdg[:, d, 0:P], src[1], mask, ALU.add).then_inc(mdiag_ready, 1)
                for i in range(QT):
                    b, full = use()
                    dve.wait_ge(*full)
                    for d in range(2):
                        c0, c1, o = tri(d, i)
                        dve.wait_ge(*seen(d_full))
                        s0 = c0 if i == 0 else c0 - P
                        dve.scalar_tensor_tensor(out=amat[:, d * AW + o:d * AW + o + c1 - c0], in0=acc[b][:, s0:s0 + c1 - c0], scalar=MD ** -0.5,
                                                 in1=two[:, d, c0:c1], op0=ALU.mult, op1=ALU.mult).then_inc(a_made, 1)
                for blk in range(MB):
                    use(False)
                for d in range(2):
                    for kt in range(4):
                        ins = dve.tensor_copy(nrep[:, kt, :], nall[:, d, head_cols(h, kt)].to_broadcast([P, P]))
                    dve.wait_ge(*seen(wb_read))
                    dve.wait_ge(*seen(eb_read))
                    for kt in range(4):
                        seen.back(dve, ("qw", kt % 2))
                        dve.tensor_tensor(mdg[:, kt % 2, 0:NS], mq[:, kt, P:T], ht[:, 1, 0:NS], ALU.mult).then_inc(qw_full, 1)
                        seen.lend(("qw", kt % 2), c_used[kt % 2])
                    bb = [use(False)[0], use(False)[0]]
                    seen.back(dve, ("qw", 1))
                    for src, c0, c1 in ((ob[0][:, :], P, T), (ob[1][:, 0:P], 0, P)):
                        step(dve.tensor_tensor(ht[:, 0, c0:c1], src, ht[:, 0, c0:c1], ALU.max))
                        step(dve.scalar_tensor_tensor(out=ht[:, 0, c0:c1], in0=src, scalar=-1.0, in1=ht[:, 0, c0:c1], op0=ALU.mult, op1=ALU.max))
                    step(dve.reciprocal(ht[:, 0, :], ht[:, 0, :]))
                    out = xm if d == 0 else mq
                    for e in range(4):
                        dve.tensor_tensor(out[:, e, P:T], acc[bb[e // 2]][:, (e % 2) * 512:(e % 2) * 512 + 512], ht[:, 0, P:T], ALU.mult)
                        ins = dve.tensor_tensor(out[:, e, 0:P], pt[:, 512 + e * P:512 + (e + 1) * P], ht[:, 0, 0:P], ALU.mult)
                    ins.then_inc(h_done, 1)
                    dve.wait_ge(*seen(h_done))
                dve.tensor_tensor(xm[:, :, 0:T], xm[:, :, 0:T], mq[:, :, :], ALU.add).then_inc(h_sum, 1)
                for d in range(2):
                    dve.tensor_scalar(two[:, d, 0:512], ktm[:, :], ccol[:, d, 5:6], MD ** -0.5, ALU.mult, ALU.mult).then_inc(kw_ready, 1)
                b, full = use()
                dve.wait_ge(*full)
                dve.wait_ge(*seen(h_sum))
                for blk in range(MB):
                    ins = dve.scalar_tensor_tensor(out=xm[:, blk, 0:T], in0=acc[b][:, AO:AO + T], scalar=-1.0 / MD, in1=xm[:, blk, 0:T],
                                                   op0=ALU.mult, op1=ALU.add)
                ins.then_inc(centred, 1)
                for _ in range(4):
                    use()
                use()
                dve.wait_ge(*seen(centred))
                dve.wait_ge(*seen(mroot_ready))
                step(dve.reciprocal(rinv[:, :], rinv[:, :]))
                for blk in range(MB):
                    ins = dve.tensor_tensor(xm[:, blk, 0:T], xm[:, blk, 0:T], rinv[:, :], ALU.mult)
                step(ins)
                for blk in range(MB):
                    ins = dve.scalar_tensor_tensor(out=xm[:, blk, 0:T], in0=xm[:, blk, 0:T], scalar=hcol[:, blk:blk + 1], in1=xc[:, blk, :],
                                                   op0=ALU.mult, op1=ALU.add)
                step(ins)
                for stored in (*c_stored, n_stored):
                    dve.wait_ge(*seen(stored, 32))
                dve.tensor_tensor(mk[:, :, :], mk[:, :, :], xm[:, :, 0:T], ALU.mult).then_inc(ym_ready, 1)
            seen.repeat(dve, MH, head_b)
            for s in range(2):
                seen(proj_done[s], 4 * MH)
            for r in range(2):
                for kt in range(KT):
                    dve.wait_ge(*seen(yhi_ready))
                    dve.tensor_tensor((hl, yl)[r][:, kt, :], yb[:, r, kt, :], (hh, yh)[r][:, kt, :].bitcast(F32), ALU.subtract).then_inc(y_ready, 1)
            for r in range(2):
                def outs(i, r=r):
                    for s in range(2):
                        add_gated(s, i * 2 + s)
                seen.repeat(dve, KT // 2, outs)
                dve.wait_ge(*seen(x_ready, KT))

        block = ctx.enter_context(nc.Block())

        @block.sync
        def _(sp):
            seen = Seen()

            def panel(slot, parts, reader):
                seen.back(sp, ("raw", slot))
                for dst, src in parts:
                    sp.dma_start(dst, src).then_inc(raw_full[slot], 16)
                seen.lend(("raw", slot), reader[slot])

            def whole(slot, w, c, reader=w_full):
                v = w_at(w, c)
                panel(slot, [(raw[:, slot, 0:4, :], v[:, 0:4, :]), (raw[:, slot, 4:8, :], v[:, 4:8, :])], reader)

            c4 = A["consts"]
            sp.dma_start(consts[:, :, :], c4[:, 0:4 * P].rearrange("p (a c) -> p a c", a=4)).then_inc(const_in, 16)
            sp.dma_start(cs[:, :, :], c4[:, 4 * P:4 * P + 2 * NS].rearrange("p (a c) -> p a c", a=2)).then_inc(const_in, 16)
            for i, n in enumerate(("q1", "k1", "q2", "k2")):
                sp.dma_start(lamr[0:1, i, :], A["diff_lambda_" + n]).then_inc(const_in, 16)
            for dst, src in row_parts(rows, A):
                sp.dma_start(dst, src).then_inc(rows_in, 16)
            for t in range(QT):
                src = A["x_prompt"][0] if t == 0 else A["x_sample"][0, (t - 1) * P:t * P, :]
                seen.back(sp, ("xin", t % 2))
                sp.dma_start(xtile[t % 2], src.rearrange("p (a c) -> p a c", a=2)).then_inc(xin_full[t % 2], 16)
                seen.lend(("xin", t % 2), acc_full[t % 2])

            for layer, kind in enumerate(kinds):
                j = layer // 3

                def mod_turn(i):
                    for s in range(6):
                        whole(s % RAW, A["w_mod"][layer], i * (6 * P) + s * P, raw_used)
                seen.repeat(sp, 4, mod_turn)

                if layer == 3:
                    sp.wait_ge(x_ready, sum(XR[:3]))
                if kind == "gqa":
                    w = A["gqa_w_in"][j]
                    ckd, cvd = (A[f"cache_gqa_{n}"][0, j].rearrange("t h d -> t (h d)") for n in "kv")

                    def group(g):
                        seen.back(sp, "ck")
                        sp.dma_start(ck[:, 0:HD], ckd[:, bass.ds(g * HD, HD)]).then_inc(cache_full, 16)
                        sp.dma_start(ck[:, HD:P], cvd[:, bass.ds(g * HD, HD)]).then_inc(cache_full, 16)
                        seen.lend("ck", v_used)
                        panel(2, [(raw[:, 2, :, 0:HD], w_at(w, g * HD + GQ_Q * HD, HD)),
                                  (raw[:, 2, :, HD:P], w_at(w, g * HD + (GQ_Q + GQ_KV) * HD, HD))], w_full)
                        whole(0, w, g * (2 * P))
                        whole(1, w, g * (2 * P) + P)
                        whole(0, w, g * (2 * P) + (GQ_Q + 2 * GQ_KV) * HD)
                        whole(1, w, g * (2 * P) + (GQ_Q + 2 * GQ_KV) * HD + P)
                    seen.repeat(sp, GQ_KV, group)
                    wo = A["gqa_w_out"][j]
                elif kind == "diff":
                    w = A["diff_w_in"][0]
                    ckd = A["cache_diff_k"][0, 0].rearrange("t h a d -> t (h a d)")
                    cvd = A["cache_diff_v"][0, 0].rearrange("t h d -> t (h d)")

                    def head(n):
                        seen.back(sp, "ck")
                        sp.dma_start(ck[:, :], ckd[:, bass.ds(n * P, P)]).then_inc(cache_full, 16)
                        for s, c in enumerate((0, D, 2 * D, 3 * D)):
                            whole(s % 2, w, n * P + c)
                        seen.back(sp, "vc")
                        sp.dma_start(vtm[:, QT, :], cvd[:, bass.ds(n * P, P)]).then_inc(vc_full, 16)
                        seen.lend("vc", v_used)
                        seen.marks["ck"] = seen.marks["vc"]
                    seen.repeat(sp, KT, head)
                    wo = A["diff_w_out"][0]
                else:
                    mlstm_sp(sp, seen, whole)
                    continue

                def outs(i):
                    for s in range(2):
                        whole(s, wo, i * (2 * P) + s * P)
                seen.repeat(sp, KT // 2, outs)

        @block.gpsimd
        def _(pool):
            seen = Seen()
            pool.memset(eps[:, :], EPS).then_inc(eps_set, 1)

            def split(s):
                pool.wait_ge(*seen(raw_full[s], 32))
                seen.back(pool, ("w", s))
                pool.tensor_tensor(idle[:, :], eps[:, :], eps[:, :], ALU.add)
                pool.tensor_copy(wh[:, s], raw[:, s]).then_inc(pool_step, 1)
                pool.wait_ge(*seen(pool_step))
                pool.tensor_tensor(wl[:, s], raw[:, s], wh[:, s].bitcast(F32), ALU.subtract).then_inc(w_full[s], 1)
                seen.lend(("w", s), proj_done[s])

            for layer, kind in enumerate(kinds):
                for s in range(RAW):
                    seen(raw_full[s], 32 * 8)
                if kind == "mlstm":
                    mlstm_pool(pool, seen, split)
                    continue

                def panels(order):
                    def turn(i):
                        for s in order:
                            split(s)
                    return turn
                seen.repeat(pool, *((GQ_KV, panels((2, 0, 1, 0, 1))) if kind == "gqa" else (KT, panels((0, 1, 0, 1)))))
                seen.repeat(pool, KT // 2, panels((0, 1)))

        @block.tensor
        def _(pe):
            seen, turn = Seen(), Turns()

            def buffer(freed_by=acc_free):
                b = turn()
                seen.back(pe, ("acc", b))
                if freed_by is None:
                    seen.marks.pop(("acc", b), None)
                else:
                    seen.lend(("acc", b), freed_by[b] if freed_by is acc_free else freed_by)
                return b

            def project(s, hi=hh, lo=hl, ready=None, freed_by=acc_free):
                b = buffer(freed_by)
                pe.wait_ge(*seen(w_full[s]))
                for kt in range(KT):
                    if ready is not None:
                        pe.wait_ge(*seen(ready))
                    for n, (w, h) in enumerate(((wh, hi), (wh, lo), (wl, hi))):
                        for t, c in halves():
                            ins = pe.matmul(acc[b][:, c:c + 320], w[:, s, kt, :], h[:, kt, t:t + 320],
                                            start=kt == 0 and n == 0, stop=kt == KT - 1 and n == 2)
                ins.then_inc(proj_done[s], 1)

            def wide(lhsT, rhs, start=True, stop=True, b=None, parts=P):
                for t, c in halves():
                    ins = pe.matmul(acc[b][0:parts, c:c + 320], lhsT, rhs[:, t:t + 320], start=start, stop=stop)
                return ins

            def sum_squares():
                b = buffer(root_ready)
                for kt in range(KT):
                    pe.wait_ge(*seen(sq_full))
                    ins = wide(ones, two[:, kt % 2, :], kt == 0, kt == KT - 1, b)
                    ins.then_inc(sq_used if kt < KT - 1 else acc_full[b], 1)

            def modulation():
                seen.back(pe, "ob1")
                def six(i):
                    for s in range(6):
                        r = s % RAW
                        pe.wait_ge(*seen(raw_full[r], 32))
                        for kt in range(KT):
                            ins = pe.matmul(ob[1][:, bass.ds(i * 12 + 2 * s, 2)], raw[:, r, kt, :],
                                            cond[:, kt:2 * KT:KT], start=kt == 0, stop=kt == KT - 1,
                                            skip_group_check=True)
                        ins.then_inc(raw_used[r], 1)
                seen.repeat(pe, 4, six)
                seen.lend("ob1", mod_ready)

            pe.wait_ge(const_in, 16 * 6)
            pe.wait_ge(rows_in, 16 * len(row_parts(rows, A)))
            for i, n in enumerate((P, 29, 112)):
                ins = pe.transpose(pt[:, i * P:i * P + n], rows[0:n, i, :], ident[0:n, 0:n])
            ins.then_inc(cols_turned, 1)
            for t in range(QT):
                b = buffer(x_in)
                pe.wait_ge(*seen(xin_full[t % 2], 16))
                for kt in range(KT):
                    ins = pe.transpose(acc[b][:, kt * P:(kt + 1) * P], xtile[t % 2][:, kt // 4, (kt % 4) * P:(kt % 4 + 1) * P], ident)
                ins.then_inc(acc_full[b], 1)
            pe.wait_ge(*seen(lam_ready))
            pe.matmul(ob[0][:, 0:1], ones[0:1, :], lamt[0:1, 4:5], start=True, stop=True).then_inc(lam_sent, 1)
            seen.lend("ob0", cols_ready)
            pe.wait_ge(*seen(cond_ready))

            def scores(k, qs, m):
                qt, _ = steps[k]
                b = buffer(None)
                q = qst[:, qs, qt * P:(qt + 1) * P]
                for c0, c1, o in ([(0, P, AO)] if qt == 0 else [(P, P + 320, AO), (P + 320, P + 640, AO + 320)]):
                    for n in range(2):
                        ins = pe.matmul(acc[b][:, o:o + c1 - c0], q, kst[:, m, n, c0:c1], start=n == 0, stop=n == 1)
                ins.then_inc(acc_full[b], 1)

            def turn_p(src, qt):
                for i in range(1 if qt == 0 else 5):
                    ins = pe.transpose(pt[:, TO + i * P:TO + (i + 1) * P], src[:, i * P:(i + 1) * P], ident)
                ins.then_inc(pt_full, 1)

            def values(slot, qt, vals, last=None):
                pe.wait_ge(*seen(pts_dve))
                if qt > 0:
                    pe.wait_ge(*seen(pts_act))
                seen.back(pe, f"ob{slot}")
                n = 1 if qt == 0 else 5
                for i in range(n):
                    ins = pe.matmul(ob[slot][:, 0:vals(0).shape[-1]], ht[:, slot, i * P:(i + 1) * P],
                                    vals(i if qt == 0 else i + 1), start=i == 0, stop=i == n - 1)
                ins.then_inc(ob_full[slot], 1)
                seen.lend(f"ob{slot}", last or ob_free[slot])

            def turn_out(end):
                b = buffer(yt_ready)
                for t in range(QT):
                    ins = pe.transpose(acc[b][:, TO + t * P:TO + (t + 1) * P], osb[:, t, :], ident)
                    if end and t == 0:
                        ins.then_inc(v_used, 1)
                ins.then_inc(acc_full[b], 1)

            def rotate(src):
                b = buffer(rot_read)
                pe.matmul(acc[b][:, 0:NS], perm, src[:, P:T], start=True, stop=True).then_inc(acc_full[b], 1)

            def head_sums(slot):
                b = buffer(nroot_ready)
                pe.wait_ge(*seen(sq_full))
                wide(half1, two[:, slot, :], b=b).then_inc(acc_full[b], 1)

            def gqa_group(g):
                first = seen.i is None
                project(2, ready=h_ready if first else None)
                project(0)
                head_sums(0)
                project(1)
                head_sums(1)
                project(0)
                pe.wait_ge(*seen(qk_scaled))
                rotate(kv)
                head_sums(0)
                project(1)
                for blk in range(2):
                    pe.wait_ge(*seen(qk_scaled))
                    rotate(qn[:, blk])
                b = buffer(tm_ready)
                for t in range(QT):
                    pe.transpose(acc[b][:, TO + t * P:TO + (t + 1) * P], kv[:, t * P:(t + 1) * P], ident)
                pe.wait_ge(*seen(cache_full, 32))
                pe.transpose(acc[b][:, TO + T:TO + T + P], ck[:, :], ident).then_inc(acc_full[b], 1)
                pe.wait_ge(*seen(st_ready))
                for blk in range(2):
                    scores(0, 2 * blk, 0)
                    scores(1, 2 * blk + 1, 0)
                    for k in range(NST):
                        pe.wait_ge(*seen(p_ready))
                        turn_p(two[:, k % 2], steps[k][0])
                        if k + 2 < NST:
                            scores(k + 2, 2 * blk + k % 2, 0)
                        values(k % 2, steps[k][0], lambda t: vtm[:, t, HD:P] if t < QT else ck[:, HD:P])
                    for o in range(2):
                        seen.back(pe, f"ob{o}")
                    turn_out(blk == 1)

            def diff_head(n):
                first = seen.i is None
                for name, s in (("q", 0), ("k", 1), ("v", 0)):
                    project(s, ready=h_ready if first and name == "q" else None, freed_by=raw_copied)
                    seen.marks[name] = seen.marks[("acc", (turn.k - 1) % 2)]
                seen.back(pe, "q")
                rotate(qn[:, 0])
                project(1)
                seen.back(pe, "k")
                rotate(kv)
                b = buffer(tm_ready)
                seen.back(pe, "v")
                for t in range(QT):
                    ins = pe.transpose(acc[b][:, TO + t * P:TO + (t + 1) * P], qn[:, 1, t * P:(t + 1) * P], ident)
                ins.then_inc(acc_full[b], 1)
                b = buffer(tm_ready)
                pe.transpose(acc[b][:, 0:P], kv[:, 0:P], ident).then_inc(acc_full[b], 1)
                b = buffer(tm_ready)
                pe.wait_ge(*seen(cache_full, 16))
                pe.transpose(acc[b][:, 0:P], ck[:, :], ident).then_inc(acc_full[b], 1)
                pe.wait_ge(*seen(st_ready))
                pe.wait_ge(*seen(vc_full, 16))
                scores(0, 0, 0)
                scores(1, 1, 1)
                for qt in range(QT):
                    pe.wait_ge(*seen(e_ready, 2))
                    if qt + 1 < QT:
                        scores(2 * qt + 2, 0, 0)
                        scores(2 * qt + 3, 1, 1)
                    pe.wait_ge(*seen(comb_ready))
                    turn_p(comb, qt)
                    values(qt % 2, qt, lambda t: vtm[:, t, :], osb_ready if qt == QT - 1 else None)
                pe.wait_ge(*seen(o_scaled))
                turn_out(True)

            for layer, kind in enumerate(kinds):
                modulation()
                sum_squares()
                if kind == "mlstm":
                    mlstm_pe(pe, seen, turn, buffer, project)
                    continue
                seen.repeat(pe, *((GQ_KV, gqa_group) if kind == "gqa" else (KT, diff_head)))
                pe.wait_ge(*seen(y_ready, KT))

                def outs(i):
                    for s in range(2):
                        project(s, yh, yl, freed_by=x_ready)
                seen.repeat(pe, KT // 2, outs)
                for s in range(RAW):
                    seen(raw_full[s], 32 * PANELS[kind][s])
            sum_squares()
            pe.wait_ge(*seen(normed))
            for t in range(QT):
                b = buffer(out_ready)
                for kt in range(KT):
                    ins = pe.transpose(acc[b][:, kt * P:(kt + 1) * P], x[:, kt, t * P:(t + 1) * P], ident)
                ins.then_inc(acc_full[b], 1)

        @block.scalar
        def _(act):
            seen, turn = Seen(), Turns()

            def use(full=True):
                b = turn()
                return (b, seen(acc_full[b])) if full else (b, None)

            def wide(b, rows=P):
                return acc[b][0:rows, AO:AO + T]

            act.wait_ge(eps_set, 1)
            act.wait_ge(*seen(cols_ready))
            act.activation(cond[:, :], cols[:, 1, 0:16], ACT.Silu).then_inc(cond_ready, 1)
            act.wait_ge(*seen(lam_sum))
            act.activation(lamt[0:1, 2:4], lamt[0:1, 0:2], ACT.Exp).then_inc(lam_exp, 1)
            for t in range(QT):
                b, full = use()
                act.wait_ge(*full)
                act.copy(x[:, :, t * P:(t + 1) * P], acc[b][:, :].rearrange("p (k c) -> p k c", c=P)).then_inc(x_in, 1)

            def norm_squares():
                for kt in range(KT):
                    if kt >= 2:
                        act.wait_ge(*seen(sq_used))
                    act.activation(two[:, kt % 2, :], x[:, kt, :], ACT.Square).then_inc(sq_full, 1)
                seen(sq_used)
                b, full = use()
                act.wait_ge(*full)
                act.activation(rinv[:, :], wide(b), ACT.Sqrt, bias=eps[:, :], scale=1.0 / D).then_inc(root_ready, 1)

            def modulate():
                act.wait_ge(*seen(mod_ready))
                for kt in range(KT):
                    s = kt % 2
                    act.wait_ge(*seen(xr_full))
                    if kt >= 2:
                        act.wait_ge(*seen(h_ready))
                    act.activation(ht[:, s, 0:P], two[:, s, 0:P], ACT.Identity, bias=mod[:, kt, 0:1], scale=amul[:, kt, 0:1])
                    act.activation(ht[:, s, P:T], two[:, s, P:T], ACT.Identity, bias=mod[:, kt, 1:2], scale=amul[:, kt, 1:2]).then_inc(xr_used, 1)
                    act.wait_ge(*seen(xr_used))
                    act.copy(hh[:, kt, :], ht[:, s, :]).then_inc(ht_full, 1)
                seen(h_ready, 2)

            def numerators(k, w, ready=p_ready):
                b, full = use()
                act.wait_ge(*seen(nb_ready))
                act.activation(two[:, k % 2, 0:w], acc[b][:, AO:AO + w], ACT.Exp, bias=st[:, k % 4, 1:2], scale=SM,
                               accum_out=st[:, k % 4, 2:3]).then_inc(ready, 1)

            def turned(slot, qt):
                full = seen(pt_full)
                if qt > 0:
                    act.wait_ge(*full)
                    act.copy(ht[:, slot, BM:T], pt[:, TO + BM:TO + T]).then_inc(pts_act, 1)

            def y_high(n):
                act.wait_ge(*seen(yt_ready))
                act.copy(yh[:, n:n + 1, :] if isinstance(n, int) else yh[:, bass.ds(n, 1), :],
                         comb[:, :].rearrange("p (a t) -> p a t", a=1)).then_inc(yhi_ready, 1)

            width = lambda qt: P if qt == 0 else T

            def gqa_group(g, j=0):
                def squares(s, slot, dst):
                    b, _ = use(False)
                    act.wait_ge(*seen(proj_done[s]))
                    act.activation(two[:, slot, :], wide(b), ACT.Square).then_inc(sq_full, 1)
                    act.copy(dst, wide(b)).then_inc(acc_free[b], 1)

                def root(slot, n):
                    b, full = use()
                    act.wait_ge(*full)
                    act.activation(ht[0:n, slot, :], wide(b, n), ACT.Sqrt, bias=eps[0:n, :], scale=1.0 / HD).then_inc(nroot_ready, 1)

                def gate(s):
                    b, _ = use(False)
                    act.wait_ge(*seen(proj_done[s]))
                    act.activation(z[:, s, :], wide(b), ACT.Silu).then_inc(acc_free[b], 1)

                squares(2, 0, kv[:, 0:T])
                squares(0, 1, qn[:, 0, :])
                root(0, HD)
                squares(1, 0, qn[:, 1, :])
                root(1, P)
                gate(0)
                use()
                act.wait_ge(*seen(qk_scaled))
                root(0, P)
                gate(1)
                use()
                use()
                b, full = use()
                act.wait_ge(*full)
                seen.back(act, "vtm0")
                seen.back(act, "kp")
                act.copy(vtm[:, 0:QT, HD:P], acc[b][:, TO:TO + T].rearrange("p (a c) -> p a c", a=QT)[:, :, HD:P])
                act.copy(kp[:, 0:HD], acc[b][:, TO:TO + HD])
                act.copy(kv[0:HD, T:T + PAST], acc[b][0:HD, TO + T:TO + T + P]).then_inc(tm_ready, 1)
                act.wait_ge(*seen(tm_ready))
                act.dma_start(O["gqa_k"][0, j].rearrange("t h d -> t (h d)")[:, bass.ds(g * HD, HD)], kp[:, 0:HD]).then_inc(store_k, 16)
                act.dma_start(O["gqa_v"][0, j].rearrange("t h d -> t (h d)")[:, bass.ds(g * HD, HD)], vtm[:, 0, HD:P]).then_inc(store_v, 16)
                seen.lend("kp", store_k, 16)
                seen.lend("vtm0", store_v, 16)
                act.wait_ge(*seen(qk_turned))
                act.copy(kst[0:HD, 0, 0, :], kv[0:HD, :])
                act.copy(kst[HD:P, 0, 0, :], kv[0:HD, :]).then_inc(hi_ready, 1)
                seen(qk_scaled, 2)
                for blk in range(2):
                    act.wait_ge(*seen(qk_turned))
                    act.copy(qst[0:HD, 2 * blk, :], qn[0:HD, blk, :])
                    act.copy(qst[HD:P, 2 * blk + 1, :], qn[HD:P, blk, :]).then_inc(hi_ready, 1)
                for blk in range(2):
                    numerators(0, P)
                    for k in range(NST):
                        if k + 1 < NST:
                            numerators(k + 1, width(steps[k + 1][0]))
                        turned(k % 2, steps[k][0])
                    use()
                    y_high(g * 2 + blk)

            def diff_head(n):
                for s, dst in ((0, qn[:, 0, :]), (1, kv[:, 0:T]), (0, qn[:, 1, :])):
                    b, _ = use(False)
                    act.wait_ge(*seen(proj_done[s]))
                    act.copy(dst, wide(b)).then_inc(raw_copied, 1)
                use()
                b, _ = use(False)
                act.wait_ge(*seen(proj_done[1]))
                act.activation(z[:, 0, :], wide(b), ACT.Silu).then_inc(acc_free[b], 1)
                use()
                b, full = use()
                act.wait_ge(*full)
                seen.back(act, "vtm0")
                act.copy(vtm[:, 0:QT, :], acc[b][:, TO:TO + T].rearrange("p (a c) -> p a c", a=QT)).then_inc(tm_ready, 1)
                b, full = use()
                act.wait_ge(*full)
                seen.back(act, "kp")
                act.copy(kp[:, :], acc[b][:, 0:P]).then_inc(tm_ready, 1)
                b, full = use()
                act.wait_ge(*full)
                act.copy(kv[:, T:T + PAST], acc[b][:, 0:P]).then_inc(tm_ready, 1)
                act.wait_ge(*seen(tm_ready, 3))
                act.dma_start(O["diff_k"][0, 0].rearrange("t h a d -> t (h a d)")[:, bass.ds(n * P, P)], kp[:, :]).then_inc(store_k, 16)
                act.dma_start(O["diff_v"][0, 0].rearrange("t h d -> t (h d)")[:, bass.ds(n * P, P)], vtm[:, 0, :]).then_inc(store_v, 16)
                seen.lend("kp", store_k, 16)
                seen.lend("vtm0", store_v, 16)
                act.wait_ge(*seen(qk_turned))
                act.copy(qst[0:HD, 0, :], qn[0:HD, 0, :])
                act.copy(qst[HD:P, 1, :], qn[HD:P, 0, :]).then_inc(hi_ready, 1)
                act.wait_ge(*seen(qk_turned))
                for m in range(2):
                    act.copy(kst[0:HD, m, 0, :], kv[HD * m:HD * m + HD, :])
                    ins = act.copy(kst[HD:P, m, 0, :], kv[HD * m:HD * m + HD, :])
                ins.then_inc(hi_ready, 1)
                numerators(0, P, e_ready)
                numerators(1, P, e_ready)
                for qt in range(QT):
                    act.wait_ge(*seen(comb_ready))
                    if qt + 1 < QT:
                        numerators(2 * qt + 2, T, e_ready)
                        numerators(2 * qt + 3, T, e_ready)
                    turned(qt % 2, qt)
                act.wait_ge(*seen(osb_ready))
                for t in range(QT):
                    ins = act.activation(two[:, 0, t * P:(t + 1) * P], osb[:, t, :], ACT.Square, accum_out=oss[:, t:t + 1])
                ins.then_inc(act_step, 1)
                act.wait_ge(*seen(act_step))
                act.activation(oss[:, 0:QT], oss[:, 0:QT], ACT.Sqrt, bias=eps[:, :], scale=1.0 / P).then_inc(oroot_ready, 1)
                use()
                y_high(n)

            act.wait_ge(*seen(x_in, QT))
            for layer, kind in enumerate(kinds):
                if layer:
                    act.wait_ge(*seen(x_ready, XR[layer - 1]))
                norm_squares()
                modulate()
                if kind == "mlstm":
                    mlstm_act(act, seen, turn, use)
                    continue
                seen.repeat(act, *((GQ_KV, lambda g: gqa_group(g, layer // 3)) if kind == "gqa" else (KT, diff_head)))
                seen(proj_done[0], KT // 2)
                seen(proj_done[1], KT // 2)
            act.wait_ge(*seen(x_ready, XR[-1]))
            norm_squares()
            for t in range(QT):
                b, full = use()
                act.wait_ge(*full)
                seen.back(act, ("y", t % 2))
                act.copy(xtile[t % 2], acc[b][:, :].rearrange("p (a c) -> p a c", a=2)).then_inc(out_ready, 1)
                act.wait_ge(*seen(out_ready))
                dst = O["y_prompt"][0] if t == 0 else O["y_sample"][0, (t - 1) * P:t * P, :]
                act.dma_start(dst.rearrange("p (a c) -> p a c", a=2), xtile[t % 2]).then_inc(y_stored[t % 2], 16)
                seen.lend(("y", t % 2), y_stored[t % 2], 16)
            for stored in (store_k, store_v, *y_stored):
                if stored.name in seen.count:
                    act.wait_ge(stored, seen.count[stored.name])

        @block.vector
        def _(dve):
            seen, turn = Seen(), Turns()

            def use(full=True):
                b = turn()
                return (b, seen(acc_full[b])) if full else (b, None)

            def step(ins):
                ins.then_inc(dve_step, 1)
                dve.wait_ge(*seen(dve_step))

            def wide(b, rows=P):
                return acc[b][0:rows, AO:AO + T]

            dve.wait_ge(*seen(cols_turned))
            for i, n in enumerate((P, 29, 112)):
                ins = dve.tensor_copy(cols[:, i, 0:n], pt[:, i * P:i * P + n])
            ins.then_inc(cols_ready, 1)
            dve.wait_ge(*seen(cols_ready))
            dve.wait_ge(const_in, 16 * 6)
            for i in range(2):
                ins = dve.tensor_tensor(lamr[0:1, 2 * i, :], lamr[0:1, 2 * i, :], lamr[0:1, 2 * i + 1, :], ALU.mult)
            step(ins)
            dve.tensor_reduce(lamt[0:1, 0:2], lamr[0:1, 0:4:2, :], AX.X, ALU.add).then_inc(lam_sum, 1)
            dve.wait_ge(*seen(lam_exp))
            dve.scalar_tensor_tensor(out=lamt[0:1, 4:5], in0=lamt[0:1, 3:4], scalar=-L1, in1=lamt[0:1, 2:3],
                                     op0=ALU.add, op1=ALU.subtract).then_inc(lam_ready, 1)
            dve.wait_ge(*seen(lam_sent))
            dve.tensor_copy(lamt[:, NLAM:NLAM + 1], ob[0][:, 0:1]).then_inc(cols_ready, 1)
            seen(cols_ready)
            dve.tensor_scalar(lamt[:, SUBS:SUBS + 1], cols[:, 1, SUBG:SUBG + 1], 1.0 - L1, None, ALU.mult).then_inc(dve_step, 1)
            seen(dve_step)
            for t in range(QT):
                use()

            def modulation(layer):
                dve.wait_ge(*seen(raw_used[2], 8))
                for g in range(2):
                    ins = dve.tensor_tensor(mod[:, :, g], ob[1][:, g:48:2], cols[:, 0, layer * 24:layer * 24 + 24], ALU.add)
                step(ins)
                for g in range(2):
                    ins = dve.scalar_tensor_tensor(out=amul[:, :, g], in0=mod[:, KT:2 * KT, g], scalar=1.0,
                                                   in1=cols[:, 0, NORMG + layer * KT:NORMG + (layer + 1) * KT], op0=ALU.add, op1=ALU.mult)
                ins.then_inc(mod_ready, 1)

            def rest(kt):
                dve.wait_ge(*seen(ht_full))
                dve.tensor_tensor(hl[:, kt, :], ht[:, kt % 2, :], hh[:, kt, :].bitcast(F32), ALU.subtract).then_inc(h_ready, 1)

            def normalise():
                use()
                dve.wait_ge(*seen(root_ready))
                step(dve.reciprocal(rinv[:, :], rinv[:, :]))
                for kt in range(KT):
                    if kt >= 2:
                        dve.wait_ge(*seen(xr_used))
                    dve.tensor_tensor(two[:, kt % 2, :], x[:, kt, :], rinv[:, :], ALU.mult).then_inc(xr_full, 1)
                    if kt >= 1:
                        rest(kt - 1)
                seen(xr_used, 2)
                rest(KT - 1)

            def rope(src, n):
                b, full = use()
                dve.wait_ge(*full)
                dve.tensor_tensor(rinv[0:n, 0:NS], acc[b][0:n, 0:NS], cs[0:n, 1, :], ALU.mult).then_inc(rot_read, 1)
                step(dve.tensor_tensor(src[0:n, P:T], src[0:n, P:T], cs[0:n, 0, :], ALU.mult))
                dve.wait_ge(*seen(rot_read))
                dve.tensor_tensor(src[0:n, P:T], src[0:n, P:T], rinv[0:n, 0:NS], ALU.add).then_inc(qk_turned, 1)
                dve.wait_ge(*seen(qk_turned))

            def minus(out, a, high):
                return dve.tensor_tensor(out, a, high.bitcast(F32), ALU.subtract)

            def stats(k, w):
                b, full = use()
                dve.wait_ge(*full)
                step(dve.tensor_reduce(st[:, k % 4, 0:1], acc[b][:, AO:AO + w], AX.X, ALU.max))
                dve.tensor_scalar(st[:, k % 4, 1:2], st[:, k % 4, 0:1], -SM, None, ALU.mult).then_inc(nb_ready, 1)

            def turned(slot, qt):
                n = P if qt == 0 else BM
                dve.wait_ge(*seen(pt_full))
                dve.tensor_copy(ht[:, slot, 0:n], pt[:, TO:TO + n]).then_inc(pts_dve, 1)

            def y_rest(n, factor):
                b, full = use()
                dve.wait_ge(*full)
                o = acc[b][:, TO:TO + T]
                if factor is None:
                    ins = dve.tensor_tensor(comb[:, :], o, z[:, n[1], :], ALU.mult)
                else:
                    ins = dve.scalar_tensor_tensor(out=comb[:, :], in0=o, scalar=factor, in1=z[:, n[1], :], op0=ALU.mult, op1=ALU.mult)
                ins.then_inc(yt_ready, 1)
                dve.wait_ge(*seen(yhi_ready))
                at = slice(n[0], n[0] + 1) if isinstance(n[0], int) else bass.ds(n[0], 1)
                minus(yl[:, at, :], comb[:, :].rearrange("p (a t) -> p a t", a=1), yh[:, at, :]).then_inc(y_ready, 1)

            width = lambda qt: P if qt == 0 else T

            def gqa_group(g, j=0):
                def scaled(slot, n, data, gain):
                    dve.wait_ge(*seen(nroot_ready))
                    step(dve.reciprocal(ht[0:n, slot, :], ht[0:n, slot, :]))
                    dve.scalar_tensor_tensor(out=data, in0=data, scalar=cols[0:n, 1, gain + j:gain + j + 1], in1=ht[0:n, slot, :],
                                             op0=ALU.mult, op1=ALU.mult).then_inc(qk_scaled, 1)

                use(False)
                use(False)
                use()
                use(False)
                use()
                use(False)
                scaled(0, HD, kv[0:HD, 0:T], KG)
                scaled(1, P, qn[:, 0, :], QG)
                rope(kv, HD)
                use()
                use(False)
                scaled(0, P, qn[:, 1, :], QG)
                rope(qn[:, 0], P)
                rope(qn[:, 1], P)
                use()
                dve.wait_ge(*seen(hi_ready))
                minus(kst[0:HD, 0, 1, :], kv[0:HD, :], kst[0:HD, 0, 0, :])
                minus(kst[HD:P, 0, 1, :], kv[0:HD, :], kst[0:HD, 0, 0, :])
                for blk in range(2):
                    dve.wait_ge(*seen(hi_ready))
                    minus(qst[HD:P, 2 * blk, :], qn[0:HD, blk, :], qst[0:HD, 2 * blk, :])
                    ins = minus(qst[0:HD, 2 * blk + 1, :], qn[HD:P, blk, :], qst[HD:P, 2 * blk + 1, :])
                ins.then_inc(st_ready, 1)

                def output(k):
                    qt, head = steps[k]
                    step(dve.reciprocal(st[:, k % 4, 3:4], st[:, k % 4, 2:3]))
                    dve.wait_ge(*seen(ob_full[k % 2]))
                    dve.tensor_scalar(osb[:, qt, head * HD:(head + 1) * HD], ob[k % 2][:, 0:HD], st[:, k % 4, 3:4], None,
                                      ALU.mult).then_inc(ob_free[k % 2], 1)

                for blk in range(2):
                    stats(0, P)
                    stats(1, P)
                    for k in range(NST):
                        turned(k % 2, steps[k][0])
                        if k + 2 < NST:
                            stats(k + 2, width(steps[k + 2][0]))
                        if k:
                            output(k - 1)
                    output(NST - 1)
                    y_rest((g * 2 + blk, blk), None)

            def diff_head(n):
                use(False)
                use(False)
                use(False)
                rope(qn[:, 0], P)
                use(False)
                rope(kv, P)
                use()
                use()
                use()
                dve.wait_ge(*seen(hi_ready))
                minus(qst[HD:P, 0, :], qn[0:HD, 0, :], qst[0:HD, 0, :])
                minus(qst[0:HD, 1, :], qn[HD:P, 0, :], qst[HD:P, 1, :])
                dve.wait_ge(*seen(hi_ready))
                for m in range(2):
                    for half in (0, HD):
                        at = slice(HD * m, HD * m + HD)
                        ins = minus(kst[half:half + HD, m, 1, :], kv[at, :], kst[at, m, 0, :])
                ins.then_inc(st_ready, 1)

                def output(qt):
                    dve.wait_ge(*seen(ob_full[qt % 2]))
                    dve.tensor_copy(osb[:, qt, :], ob[qt % 2][:, 0:P]).then_inc(osb_ready if qt == QT - 1 else ob_free[qt % 2], 1)

                stats(0, P)
                stats(1, P)
                for qt in range(QT):
                    w, k = width(qt), 2 * qt
                    dve.wait_ge(*seen(e_ready, 2))
                    dve.reciprocal(st[:, k % 4, 3:4], st[:, k % 4, 2:3])
                    step(dve.reciprocal(st[:, k % 4 + 1, 3:4], st[:, k % 4 + 1, 2:3]))
                    step(dve.tensor_scalar(st[:, k % 4 + 1, 4:5], st[:, k % 4 + 1, 3:4], lamt[:, NLAM:NLAM + 1], None, ALU.mult))
                    step(dve.tensor_scalar(two[:, 1, 0:w], two[:, 1, 0:w], st[:, k % 4 + 1, 4:5], None, ALU.mult))
                    dve.scalar_tensor_tensor(out=comb[:, 0:w], in0=two[:, 0, 0:w], scalar=st[:, k % 4, 3:4], in1=two[:, 1, 0:w],
                                             op0=ALU.mult, op1=ALU.add).then_inc(comb_ready, 1)
                    if qt + 1 < QT:
                        stats(k + 2, T)
                        stats(k + 3, T)
                    turned(qt % 2, qt)
                    if qt:
                        output(qt - 1)
                output(QT - 1)
                dve.wait_ge(*seen(oroot_ready))
                step(dve.reciprocal(oss[:, 0:QT], oss[:, 0:QT]))
                for t in range(QT):
                    ins = dve.tensor_scalar(osb[:, t, :], osb[:, t, :], oss[:, t:t + 1], None, ALU.mult)
                ins.then_inc(o_scaled, 1)
                y_rest((n, 0), lamt[:, SUBS:SUBS + 1])

            def add_gated(s, n):
                b, _ = use(False)
                dve.wait_ge(*seen(proj_done[s]))
                at = slice(n, n + 1) if isinstance(n, int) else bass.ds(n, 1)
                gt = slice(n + 16, n + 17) if isinstance(n, int) else bass.ds(n + 16, 1)
                for g, (c0, c1) in enumerate(((0, P), (P, T))):
                    ins = dve.scalar_tensor_tensor(
                        out=x[:, at, c0:c1], in0=acc[b][:, AO + c0:AO + c1].rearrange("p (a t) -> p a t", a=1),
                        scalar=mod[:, gt, g], in1=x[:, at, c0:c1], op0=ALU.mult, op1=ALU.add)
                ins.then_inc(x_ready, 1)

            for layer, kind in enumerate(kinds):
                modulation(layer)
                normalise()
                if kind == "mlstm":
                    mlstm_dve(dve, seen, turn, use, step, add_gated)
                    continue
                for s in range(3):
                    seen(proj_done[s], PANELS[kind][s] - (KT // 2 if s < 2 else 0))
                seen.repeat(dve, *((GQ_KV, lambda g: gqa_group(g, layer // 3)) if kind == "gqa" else (KT, diff_head)))

                def outs(i):
                    for s in range(2):
                        add_gated(s, i * 2 + s)
                seen.repeat(dve, KT // 2, outs)
                dve.wait_ge(*seen(x_ready, KT))
            use()
            dve.wait_ge(*seen(root_ready))
            step(dve.reciprocal(rinv[:, :], rinv[:, :]))
            for kt in range(KT):
                ins = dve.scalar_tensor_tensor(out=x[:, kt, :], in0=x[:, kt, :], scalar=cols[:, 1, FING + kt:FING + kt + 1],
                                               in1=rinv[:, :], op0=ALU.mult, op1=ALU.mult)
            ins.then_inc(normed, 1)


def row_parts(rows, A):
    v = lambda a, pat="(b p) -> b p": a.rearrange(pat, p=P)
    parts = [(rows[0:96, 0, :], v(A["b_mod"], "l (b p) -> (l b) p")),
             (rows[96:128, 0, :], v(A["norm_g"], "l (b p) -> (l b) p")),
             (rows[0:8, 1, :], v(A["c_ctx"])),
             (rows[8:16, 1, :], v(A["c"][0])),
             (rows[16:24, 1, :], v(A["final_norm_g"]))]
    for i, name in ((24, "gqa_q_norm_g"), (26, "gqa_k_norm_g")):
        parts += [(rows[i:i + 2, 1, h * HD:(h + 1) * HD], A[name]) for h in range(2)]
    parts += [(rows[28:29, 1, :], A["diff_subln_g"]),
              (rows[0:16, 2, :], v(A["mlstm_conv_b"][0])),
              (rows[16:80, 2, :], v(A["mlstm_conv_w"][0], "k (b p) -> (k b) p")),
              (rows[80:96, 2, :], v(A["mlstm_mh_norm_g"][0])),
              (rows[96:112, 2, :], v(A["mlstm_skip"][0]))]
    return parts


def constants():
    ident = np.eye(P, dtype=np.float32)
    half = np.kron(np.eye(2), np.ones((HD, HD))).astype(np.float32)
    perm = np.zeros((P, P), np.float32)
    for m in range(P):
        d = m % HD
        perm[m + HD // 2 if d < HD // 2 else m - HD // 2, m] = -1.0 if d < HD // 2 else 1.0
    tok = np.arange(NS)
    inv = (np.float32(10000.0) ** (-np.arange(HD // 4, dtype=np.float32) / np.float32(HD // 4))).astype(np.float32)
    row, col = (tok // 64).astype(np.float32), (tok % 64).astype(np.float32)
    ang = np.concatenate([row[:, None] * inv, col[:, None] * inv], axis=-1)
    table = lambda f: np.tile(f(ang).astype(np.float32).T, (P // (HD // 2), 1))
    place = np.zeros((P, P), np.float32)
    for h in range(MH):
        for d in range(2):
            place[8 * d + h, 32 * d + h] = place[8 * d + MH + h, 64 + 32 * d + h] = 1.0
    head4 = np.kron(np.eye(P // 4), np.ones((4, 4))).astype(np.float32)
    s, t = np.mgrid[0:P, 0:P]
    masks = [(1e30 * late).astype(np.float32) for late in (t < s, t > s)]
    return np.concatenate([ident, np.ones((P, P), np.float32), half, perm, table(np.cos), table(np.sin),
                           place, head4, *masks], axis=1)


_OUTS = {"y_prompt": (1, NP_, D), "y_sample": (1, NS, D), "gqa_k": (1, 2, NP_, GQ_KV, HD), "gqa_v": (1, 2, NP_, GQ_KV, HD),
         "diff_k": (1, 1, NP_, 8, 2, HD), "diff_v": (1, 1, NP_, 8, P),
         "mlstm_C": (1, 1, 2, MH, MD, MD), "mlstm_n": (1, 1, 2, MH, MD), "mlstm_m": (1, 1, 2, MH)}


def kernel(**inputs):
    import concourse.bacc as _bacc
    from concourse.bass_utils import run_bass_kernel_spmd as _run

    nc = _bacc.Bacc("TRN2", target_bir_lowering=False, num_devices=1)
    arrays, A = {}, {}
    for name, a in {**inputs, "consts": constants()}.items():
        arrays[f"in_{name}"] = a = np.ascontiguousarray(a)
        A[name] = nc.dram_tensor(f"in_{name}", a.shape, mybir.dt.from_np(a.dtype), kind="ExternalInput").ap()
    O = {n: nc.dram_tensor(f"out_{n}", s, F32, kind="ExternalOutput").ap() for n, s in _OUTS.items()}
    scratch = {n: nc.dram_tensor(f"scratch_{n}", s, F32, kind="Internal").ap()
               for n, s in (("xm", (MH, MB, P, T + 5)), ("xc", (MH, MB, P, T)), ("y", (MH * MB, P, T)))}
    build(nc, A, O, scratch)
    r = _run(nc, [arrays], core_ids=[0])
    return tuple(r.results[0][f"out_{n}"] for n in _OUTS)
```

```python
import math
from contextlib import ExitStack

import numpy as np
import concourse.bass as bass
from concourse import mybir

F32 = mybir.dt.float32
F32R = mybir.dt.float32r
ALU = mybir.AluOpType
ACT = mybir.ActivationFunctionType
AX = mybir.AxisListType

P = 128
D = 1024
KT = D // P
NP_, NS = 128, 512
T = NP_ + NS
PAST = 128
HD = 64
DEPTH = 4
EPS = 1e-6
SM = HD ** -0.5
AO = 192
TO = 128
QT = T // P
GQ_KV = 4
GQ_Q = 16
MI = 2048
MH = 4
MD = MI // MH
MB = MD // P
RAW, SPL = 3, 3


class Seen:

    def __init__(self):
        self.count, self.per, self.marks, self.i = {}, {}, {}, None

    def value(self, name, count):
        per = self.per.get(name, 0) if self.i is not None else 0
        return self.i * per + count if per else count

    def __call__(self, sem, by=1):
        self.count[sem.name] = self.count.get(sem.name, 0) + by
        return sem, self.value(sem.name, self.count[sem.name])

    def lend(self, buffer, sem, by=1):
        self.count[sem.name] = self.count.get(sem.name, 0) + by
        self.marks[buffer] = (sem, self.count[sem.name])

    def back(self, eng, buffer):
        if buffer in self.marks:
            sem, count = self.marks[buffer]
            eng.wait_ge(sem, self.value(sem.name, count))

    def repeat(self, eng, times, body):
        start = dict(self.count)
        body(0)
        per = {k: v - start.get(k, 0) for k, v in self.count.items()}
        if times > 1:
            self.marks = {k: (s, c - per[s.name]) for k, (s, c) in self.marks.items()}
            with eng.Fori(1, times) as i:
                self.count, self.per, self.i = {k: start.get(k, 0) for k in per}, per, i
                body(i)
            self.i = None
            again = {k: v - start.get(k, 0) for k, v in self.count.items()}
            assert all(v in (0, per[k]) for k, v in again.items())
            self.marks = {k: (s, c + (times - 1) * per[s.name]) for k, (s, c) in self.marks.items()}
        self.count = {k: start.get(k, 0) + per[k] + (times - 1) * (again[k] if times > 1 else 0) for k in per}


class Turns:

    def __init__(self):
        self.k = 0

    def __call__(self):
        self.k += 1
        return (self.k - 1) % 2


def halves():
    return ((0, AO), (320, AO + 320))


def lambda_init(layer):
    return 0.8 - 0.6 * math.exp(-0.3 * layer)


def build(nc, A, O, scratch):
    kinds = ["gqa", "diff", "mlstm", "gqa"]
    with ExitStack() as ctx:
        def sb(name, shape, dt=F32, c=None):
            return (c or ctx).enter_context(nc.sbuf_tensor(name, shape, dt))

        def sem(name):
            return ctx.enter_context(nc.semaphore(name))

        x = sb("x", [P, KT, T])
        hh = sb("hh", [P, KT, T], F32R)
        hl = sb("hl", [P, KT, T], F32R)
        raw = sb("raw", [P, RAW, KT, P])
        wh = sb("wh", [P, SPL, KT, P], F32R)
        wl = sb("wl", [P, SPL, KT, P], F32R)
        consts = sb("consts", [P, 4, P])
        ident, ones, half1, perm = (consts[:, i, :] for i in range(4))
        cols = sb("cols", [P, 3, P])
        cond = sb("cond", [P, 2 * KT])
        mod = sb("mod", [P, 24, 2])
        amul = sb("amul", [P, KT, 2])
        rinv = sb("rinv", [P, T])
        two = sb("two", [P, 2, T])
        ht = sb("ht", [P, 2, T])
        eps = sb("eps", [P, 2])
        idle = sb("idle", [P, 1])
        cs = sb("cs", [P, 2, NS])

        NORMG = 96
        FING, QG, KG, SUBG = 16, 24, 26, 28
        CONVB, CONVW, MHG, SKIP = 0, 16, 80, 96

        att = ExitStack()
        yh = sb("yh", [P, KT, T], F32R, att)
        yl = sb("yl", [P, KT, T], F32R, att)
        z = sb("z", [P, 2, T], F32, att)
        kv = sb("kv", [P, T + PAST], F32, att)
        qn = sb("qn", [P, 2, T], F32, att)
        kst = sb("kst", [P, 2, 2, T + PAST], F32R, att)
        qst = sb("qst", [P, 4, T], F32R, att)
        vtm = sb("vtm", [P, QT + 1, P], F32, att)
        ck = sb("ck", [P, P], F32, att)
        kp = sb("kp", [P, P], F32, att)
        comb = sb("comb", [P, T], F32, att)
        osb = sb("osb", [P, QT, P], F32, att)
        st = sb("st", [P, 4, 16], F32, att)
        lamr = sb("lamr", [P, 4, HD], F32, att)
        lamt = sb("lamt", [P, 8], F32, att)
        oss = sb("oss", [P, 8], F32, att)
        att.close()

        AW = 11 * P
        ml = ExitStack()
        xm = sb("xm", [P, MB, T + 5], F32, ml)
        xc = sb("xc", [P, MB, T], F32, ml)
        wsm = sb("wsm", [P, 3, MI // P + MB, 4], F32, ml)
        bd = sb("bd", [P, 3, MB, P], F32, ml)
        gbias = sb("gbias", [P, 16], F32, ml)
        mc = sb("mc", [P, 4 * P], F32, ml)
        place, headmask = mc[0:16, 0:P], mc[:, P:2 * P]
        m0 = sb("m0", [64, 1], F32, ml)
        nml = sb("nml", [64, 1], F32, ml)
        mnew = sb("mnew", [64, 1], F32, ml)
        mrow = sb("mrow", [64, T], F32, ml)
        bmrow = sb("bmrow", [64, T], F32, ml)
        wirow = sb("wirow", [64, T], F32, ml)
        ct = sb("ct", [P, 6, 64], F32, ml)
        ccol = sb("ccol", [P, 2, 6], F32, ml)
        sel = sb("sel", [64, 2, P], F32, ml)
        hcol = sb("hcol", [P, 24], F32, ml)
        nall = sb("nall", [P, 2, MI // P], F32, ml)
        flag = sb("flag", [P, 1], F32, ml)
        first = ExitStack()
        crow = sb("crow", [64, T], F32, first)
        rones = sb("rones", [64, T], F32, first)
        wg = sb("wg", [P, 3 * MI // P, 16], F32, first)
        bdt = sb("bdt", [P, 12, P], F32, first)
        gm = sb("gm", [P, MB, 32], F32, first)
        cv = sb("cv", [P, 2, T + 5], F32, first)
        nrow = sb("nrow", [2 * MI // P, P], F32, first)
        g16 = sb("g16", [16, T], F32, first)
        r1 = sb("r1", [64, T], F32, first)
        r2 = sb("r2", [64, T], F32, first)
        first.close()
        second = ExitStack()
        mq = sb("mq", [P, MB, T], F32, second)
        mk = sb("mk", [P, MB, T], F32, second)
        mv = sb("mv", [P, QT, MD], F32, second)
        ktm = sb("ktm", [P, MD], F32, second)
        amat = sb("amat", [P, 2 * AW], F32, second)
        mdg = sb("mdg", [P, 2, T], F32, second)
        nrep = sb("nrep", [P, MB, P], F32, second)
        second.close()
        ml.close()

        def cst(u):
            return amat[:, u * 1024:(u + 1) * 1024].rearrange("p (a c) -> p a c", a=2)

        def nst(d):
            return mdg[0:1, d, 0:MD]

        back = ExitStack()
        sb("under_yh_yl", [P, 2, KT, T], F32, back)
        yb = sb("yb", [P, 2, KT, T], F32, back)
        back.close()

        acc = [ctx.enter_context(nc.psum_tensor(f"acc{b}", [P, 1024], F32)) for b in range(2)]
        pt = ctx.enter_context(nc.psum_tensor("pt", [P, 1024], F32))
        ob = [ctx.enter_context(nc.psum_tensor(f"ob{b}", [P, 512], F32)) for b in range(2)]

        raw_full = [sem(f"raw_full{s}") for s in range(RAW)]
        raw_used = [sem(f"raw_used{s}") for s in range(RAW)]
        w_full = [sem(f"w_full{s}") for s in range(SPL)]
        proj_done = [sem(f"proj_done{s}") for s in range(SPL)]
        acc_full = [sem(f"acc_full{b}") for b in range(2)]
        acc_free = [sem(f"acc_free{b}") for b in range(2)]
        ob_full = [sem(f"ob_full{b}") for b in range(2)]
        ob_free = [sem(f"ob_free{b}") for b in range(2)]
        xin_full = [sem(f"xin_full{b}") for b in range(2)]
        y_stored = [sem(f"y_stored{b}") for b in range(2)]
        names = """const_in rows_in eps_set cols_turned cols_ready cond_ready x_in x_ready lam_sum lam_exp lam_ready
            lam_sent pool_step act_step dve_step sq_full sq_used root_ready mod_ready xr_full xr_used ht_full h_ready
            nroot_ready qk_scaled rot_read qk_turned hi_ready st_ready raw_copied cache_full vc_full v_used
            nb_ready p_ready e_ready comb_ready pts_dve pts_act pt_full osb_ready oroot_ready o_scaled yt_ready yhi_ready y_ready
            tm_ready store_k store_v normed out_ready""".split()
        (const_in, rows_in, eps_set, cols_turned, cols_ready, cond_ready, x_in, x_ready, lam_sum, lam_exp,
         lam_ready, lam_sent, pool_step, act_step, dve_step, sq_full, sq_used, root_ready, mod_ready, xr_full, xr_used,
         ht_full, h_ready, nroot_ready, qk_scaled, rot_read, qk_turned, hi_ready, st_ready, raw_copied, cache_full,
         vc_full, v_used, nb_ready, p_ready, e_ready, comb_ready, pts_dve, pts_act, pt_full, osb_ready, oroot_ready,
         o_scaled, yt_ready, yhi_ready, y_ready, tm_ready, store_k, store_v, normed, out_ready) = map(sem, names)

        names = """m_begin m_end m_in m_zeroed m_ones bd_ready bt_ready gm_ready xm_copied xc_done cv_ready gates_done
            spill g_full g_copied row_read ln_ready mact_step m_made rows_ready xm_full xc_full qkv_copied mb_full mdiag_ready
            d_full a_made bc_read z_made den_full den_read skip_made skip_added qw_full h_done h_sum centred kw_ready cst_copied n_full
            n_copied n_stored msq_full msq_used mroot_ready ym_ready y_spill m_stored""".split()
        (m_begin, m_end, m_in, m_zeroed, m_ones, bd_ready, bt_ready, gm_ready, xm_copied, xc_done, cv_ready, gates_done,
         spill, g_full, g_copied, row_read, ln_ready, mact_step, m_made, rows_ready, xm_full, xc_full, qkv_copied, mb_full, mdiag_ready,
         d_full, a_made, bc_read, z_made, den_full, den_read, skip_made, skip_added, qw_full, h_done, h_sum, centred, kw_ready, cst_copied, n_full,
         n_copied, n_stored, msq_full, msq_used, mroot_ready, ym_ready, y_spill, m_stored) = map(sem, names)
        c_full = [sem(f"c_full{b}") for b in range(2)]
        c_used = [sem(f"c_used{b}") for b in range(2)]
        c_stored = [sem(f"c_stored{b}") for b in range(2)]
        yb_full = [sem(f"yb_full{h}") for h in range(MH)]

        rows = rinv[:, 0:3 * P].rearrange("p (a c) -> p a c", a=3)
        xtile = [two[:, :, 0:512], ht[:, :, 0:512]]
        NLAM, SUBS = 5, 6
        L1 = lambda_init(1)
        BM = P * 3

        def w_at(w, c, n=P):
            return w.rearrange("(kt p) c -> p kt c", p=P)[:, :, bass.ds(c, n)]

        XR = [2 * KT if kind == "mlstm" else KT for kind in kinds]
        MODS = {None: ((8, 8, 8), 2), "gqa": ((8, 8, 8), 1), "diff": ((0, 0, 24), 2), "mlstm": ((12, 12, 0), 1)}
        MO = 256
        steps = [(qt, j) for qt in range(QT) for j in range(2)]
        NST = len(steps)

        def head_cols(h, n):
            return slice(h * MB + n, h * MB + n + 1) if isinstance(h, int) else bass.ds(h * MB + n, 1)

        def xm_at(blk, c0, c1):
            o = 2 if c1 <= P else 4
            return xm[:, blk, c0 + o:c1 + o]

        GROUPS = ((P, T, 0), (0, P, 512))

        def tri(d, i):
            if i == 0:
                return 0, P, 0
            s = i - 1
            before = sum((4 - u) if d == 0 else (u + 1) for u in range(s))
            return ((P + s * P, T) if d == 0 else (P, P + (s + 1) * P)) + ((1 + before) * P,)

        def mlstm_sp(sp, seen, whole, mod_panel):
            w = A["mlstm_w_in"][0]
            def small_operands():
                sp.wait_ge(m_begin, 1)
                for i, name in enumerate(("mlstm_w_q", "mlstm_w_k", "mlstm_w_v")):
                    sp.dma_start(wsm[:, i, 0:MI // P, :], A[name][0].rearrange("(b n) c d -> (n c) b d", n=32)).then_inc(m_in, 16)
                for g, name in enumerate("fb"):
                    sp.dma_start(wg[:, :, g * 8:(g + 1) * 8], A[f"mlstm_w_gate_{name}"][0].rearrange("(b p) c -> p b c", p=P)).then_inc(m_in, 16)
                    sp.dma_start(gbias[0:1, g * 8:(g + 1) * 8], A[f"mlstm_b_gate_{name}"]).then_inc(m_in, 16)
                sp.dma_start(mc[:, :], A["consts"][:, 4 * P + 2 * NS:]).then_inc(m_in, 16)
                sp.dma_start(nrow[:, :], A["state_mlstm_n"][0, 0].rearrange("d h (k p) -> (d h k) p", p=P)).then_inc(m_in, 16)
                sp.wait_ge(m_zeroed, 1)
                for d in range(2):
                    sp.dma_start(m0[32 * d:32 * d + MH, :], A["state_mlstm_m"][0, 0, d].rearrange("(h a) -> h a", a=1)).then_inc(m_in, 16)

            def head_a(h):
                for blk in range(MB):
                    if blk == 2 and seen.i is None:
                        small_operands()
                    whole(blk % 2, w, h * (MB * P) + blk * P)
            seen.repeat(sp, MH, head_a)
            seen.back(sp, ("raw", 2))

            sp.wait_ge(spill, 32 * MH)
            sp.wait_ge(gates_done, MH)
            cd = A["state_mlstm_C"][0, 0].rearrange("d h (k p) e -> d p h k e", p=P)

            def head_b(h):
                def gate_panel(blk):
                    whole(blk % 2, w, h * (MB * P) + blk * P + MI)

                seen.back(sp, "xc")
                sp.dma_start(xc[:, :, :], scratch["xc"][bass.ds(h, 1)].rearrange("a b p t -> p (a b) t")).then_inc(xc_full, 16)
                seen.lend("xc", skip_made)
                seen.back(sp, "xm")
                sp.dma_start(xm[:, :, :], scratch["xm"][bass.ds(h, 1)].rearrange("a b p t -> p (a b) t")).then_inc(xm_full, 16)
                seen.lend("xm", skip_added)
                gate_panel(0)
                gate_panel(1)
                for d in range(2):
                    for kt in range(4):
                        s = kt % 2
                        seen.back(sp, ("c", s))
                        sp.dma_start(raw[:, 2, 4 * s:4 * s + 4, :],
                                     cd[d][:, bass.ds(h, 1), kt, :].rearrange("p a (b e) -> p (a b) e", b=4)).then_inc(c_full[s], 16)
                        seen.lend(("c", s), c_used[s])
                    for m in range(3 * d, 3 * d + 3):
                        mod_panel(3, m % 2, h * (6 * P) + m * P)
                gate_panel(2)
                gate_panel(3)
            seen.repeat(sp, MH, head_b)

            def load_y():
                sp.wait_ge(y_spill, 16 * MH)
                sp.wait_ge(m_end, 1)
                for h in range(MH):
                    sp.dma_start(yb[:, h // 2, h % 2 * MB:h % 2 * MB + MB, :],
                                 scratch["y"][h * MB:(h + 1) * MB].rearrange("b p t -> p b t")).then_inc(yb_full[h], 16)
            wo = A["mlstm_w_out"][0]
            for r in range(2):
                def outs(i, r=r):
                    for s in range(2):
                        whole(s, wo[r * D:(r + 1) * D, :], i * (2 * P) + s * P)
                    if r == 0 and seen.i is None:
                        load_y()
                seen.repeat(sp, KT // 2, outs)

        def mlstm_pool(pool, seen, split, mod_panels):
            pool.wait_ge(m_begin, 1)
            pool.memset(m0[:, :], 0.0).then_inc(m_zeroed, 1)

            def four(i):
                for s in (0, 1, 0, 1):
                    split(s)
            def gates(h):
                for turn in range(2):
                    split(0)
                    split(1)
                    if turn == 0:
                        mod_panels(3, (3, 3))
            seen.repeat(pool, MH, four)
            seen.repeat(pool, MH, gates)
            seen.repeat(pool, 4, four)

        def mlstm_pe(pe, seen, turn, buffer, project, mod_panel, pool_takes):
            def pair(dst, lhsT, src, start, stop):
                for c0, c1, o in GROUPS:
                    ins = pe.matmul(dst(o, c1 - c0), lhsT, src(c0, c1), start=start, stop=stop, skip_group_check=True)
                return ins

            pe.wait_ge(m_in, 16 * 11)

            def head_a(h):
                project(0, ready=h_ready if seen.i is None else None, freed_by=xm_copied)
                pe.wait_ge(*seen(bd_ready))
                b = buffer(bt_ready)
                for n in range(8):
                    ins = pe.transpose(acc[b][:, n * P:(n + 1) * P], bd[:, n // 4, n % 4, :], ident)
                ins.then_inc(acc_full[b], 1)
                b = buffer(bt_ready)
                for n in range(4):
                    ins = pe.transpose(acc[b][:, n * P:(n + 1) * P], bd[:, 2, n, :], ident)
                ins.then_inc(acc_full[b], 1)
                seen.marks["bt"] = seen.marks[("acc", b)]
                project(1, freed_by=xm_copied)
                b = buffer(gm_ready)
                seen.marks["gm"] = seen.marks[("acc", b)]
                seen.back(pe, "bt")
                for blk in range(MB):
                    for n in range(3):
                        ins = pe.matmul(acc[b][:, blk * 32 + 16 * (n // 2):blk * 32 + 16 * (n // 2) + 16], bdt[:, n * 4 + blk, :],
                                        wg[:, head_cols(h, n * 16 + blk), :].rearrange("p a c -> p (a c)"),
                                        start=n != 1, stop=n != 0, skip_group_check=True)
                ins.then_inc(acc_full[b], 1)
                for s in (0, 1):
                    project(s, freed_by=xm_copied)
                turn()
                seen.back(pe, "gm")
                for blk in range(MB):
                    pe.wait_ge(*seen(xc_done))
                    first = seen.i is None and blk == 0
                    pair(lambda o, w: pt[0:16, o:o + w], gm[:, blk, 0:16], lambda c0, c1: xc[:, blk, c0:c1], first, False)
                    ins = pair(lambda o, w: pt[0:16, o:o + w], gm[:, blk, 16:32], lambda c0, c1: xm_at(blk, c0, c1), False, False)
                ins.then_inc(gates_done, 1)
            seen.repeat(pe, MH, head_a)
            pool_takes(2 * MH, 2 * MH)

            pe.wait_ge(*seen(m_ones))
            pair(lambda o, w: pt[0:16, o:o + w], gbias[0:1, :], lambda c0, c1: rones[0:1, c0:c1], False, True).then_inc(g_full, 1)
            seen.lend("pt", g_copied)
            seen.back(pe, "pt")
            for n in range(2):
                b = buffer(row_read)
                pair(lambda o, w: acc[b][0:64, o:o + w], place[:, n * 64:n * 64 + 64], lambda c0, c1: g16[0:16, c0:c1], True, True)\
                    .then_inc(acc_full[b], 1)
            b = buffer(row_read)
            pe.wait_ge(*seen(rows_ready))
            for n in range(6):
                src = crow[:, n * P:(n + 1) * P] if n < 5 else wirow[:, 0:P]
                pe.transpose(acc[b][:, n * 64:(n + 1) * 64], src, ident[0:64, 0:64])
            ins = pe.transpose(acc[b][:, 384:416], nrow[:, :], ident[0:32, 0:32])
            ins.then_inc(acc_full[b], 1)

            def full_width(b, lhsT, src, start=True, stop=True):
                for t, c in halves():
                    ins = pe.matmul(acc[b][:, c:c + 320], lhsT, src[:, t:t + 320], start=start, stop=stop)
                return ins

            def head_b(h):
                pool_takes(1, 1)
                pe.wait_ge(*seen(bd_ready))
                for d in range(2):
                    for buf in (("pt",), ("ob0", "ob1"))[d]:
                        seen.back(pe, buf)
                    dst = (lambda o, w: pt[:, o:o + w]) if d == 0 else (lambda o, w: ob[o // 512][:, 0:w])
                    pair(dst, sel[:, d, :], lambda c0, c1: mrow[:, c0:c1], True, True).then_inc(mb_full, 1)
                seen.lend("pt", d_full, 10)
                seen.marks["ob0"] = seen.marks["ob1"] = seen.marks["pt"]
                pe.wait_ge(*seen(xc_full, 16))
                for n in range(2):
                    for blk in range(MB):
                        b = buffer(qkv_copied)
                        full_width(b, bd[:, n, blk, :], xc[:, blk, :]).then_inc(acc_full[b], 1)
                pe.wait_ge(*seen(xm_full, 16))
                for tiles in ((0, 1), (2, 3), (4, 5)):
                    b = buffer(qkv_copied)
                    for u, t in enumerate(tiles):
                        for blk in range(MB):
                            lhsT = xc[:, blk, 0:P] if t == 5 else xm_at(blk, t * P, (t + 1) * P)
                            ins = pe.matmul(acc[b][:, u * 512 + blk * P:u * 512 + (blk + 1) * P], lhsT,
                                            bd[:, 1 if t == 5 else 2, blk, :], start=True, stop=True)
                    ins.then_inc(acc_full[b], 1)
                seen.marks["qkv"] = seen.marks[("acc", b)]
                seen.back(pe, "qkv")
                for i in range(QT):
                    b = buffer(None)
                    seen.lend(("acc", b), a_made, 2)
                    seen.marks["a"] = seen.marks[("acc", b)]
                    r = (0, P) if i == 0 else (P, T)
                    for kt in range(4):
                        ins = pe.matmul(acc[b][:, 0:r[1] - r[0]], mk[:, kt, i * P:(i + 1) * P], mq[:, kt, r[0]:r[1]],
                                        start=kt == 0, stop=kt == 3)
                    ins.then_inc(acc_full[b], 1)
                for d in range(2):
                    for row in (bmrow, wirow):
                        b = buffer(bc_read)
                        full_width(b, sel[:, d, :], row).then_inc(acc_full[b], 1)
                seen.back(pe, "a")
                seen.back(pe, "pt")
                for d in range(2):
                    bb = [buffer(None), buffer(None)]
                    seen.lend("num", h_done)
                    for buf in (("acc", 0), ("acc", 1), "ob0", "ob1", "pt"):
                        seen.marks[buf] = seen.marks["num"]
                    num = lambda e: acc[bb[e // 2]][:, (e % 2) * 512:(e % 2) * 512 + 512]
                    pe.matmul(ob[1][:, 0:P], ones, amat[:, d * AW:d * AW + P], start=True, stop=True)
                    for e in range(4):
                        pe.matmul(pt[:, 512 + e * P:512 + (e + 1) * P], mv[:, 0, e * P:(e + 1) * P], amat[:, d * AW:d * AW + P],
                                  start=True, stop=True, skip_group_check=True)
                    order = range(1, 5) if d == 0 else range(4, 0, -1)
                    for n, i in enumerate(order):
                        c0, c1, o = tri(d, i)
                        a = amat[:, d * AW + o:d * AW + o + c1 - c0]
                        for e in range(4):
                            pe.matmul(num(e)[:, c0 - P:c1 - P], mv[:, i, e * P:(e + 1) * P], a, start=n == 0, stop=False,
                                      skip_group_check=True)
                        pe.matmul(ob[0][:, c0 - P:c1 - P], ones, a, start=n == 0, stop=False, skip_group_check=True)
                    def initial_n(kt):
                        pe.wait_ge(*seen(qw_full))
                        return pe.matmul(ob[0][:, :], nrep[:, kt, :], mdg[:, kt % 2, 0:NS], start=False, stop=kt == 3,
                                         skip_group_check=True)

                    for kt in range(4):
                        s = kt % 2
                        if kt < 3:
                            initial_n(kt)
                        pe.wait_ge(*seen(c_full[s], 16))
                        for e in range(4):
                            if kt == 2 and e == 2:
                                initial_n(3).then_inc(den_full, 1)
                            ins = pe.matmul(num(e), raw[:, 2, 4 * s + e, :], mdg[:, s, 0:NS], start=False, stop=kt == 3, skip_group_check=True)
                        ins.then_inc(c_used[s], 1)
                    pe.wait_ge(*seen(den_read))
                    for m in range(3 * d, 3 * d + 3):
                        mod_panel(3, m % 2, h * 6 + m)
                    seen.back(pe, "num")
                pool_takes(1, 1)

                def state(d):
                    for u in range(2):
                        b = buffer(cst_copied)
                        for v in range(2):
                            kb = 2 * u + v
                            ins = pe.matmul(acc[b][:, v * 512:v * 512 + 512], ht[:, d, kb * P:(kb + 1) * P], mv[:, 0, :], start=True, stop=True)
                        ins.then_inc(acc_full[b], 1)
                    return pe.matmul((ob[0], pt)[d][0:1, 0:MD], ones[:, 0:1], ht[:, d, 0:MD], start=True, stop=True)

                pe.wait_ge(*seen(kw_ready, 2))
                state(0)
                pe.wait_ge(*seen(h_sum))
                b = buffer(centred)
                for blk in range(MB):
                    ins = full_width(b, ones, mk[:, blk, :], blk == 0, blk == 3)
                ins.then_inc(acc_full[b], 1)
                project(0, freed_by=z_made)
                project(1, freed_by=z_made)
                state(1).then_inc(n_full, 1)
                seen.lend("ob0", n_copied)
                seen.marks["pt"] = seen.marks["ob0"]
                b = buffer(mroot_ready)
                for blk in range(MB):
                    pe.wait_ge(*seen(msq_full))
                    ins = full_width(b, ones, two[:, blk % 2, :], blk == 0, blk == 3)
                    ins.then_inc(msq_used if blk < 3 else acc_full[b], 1)
                project(0, freed_by=z_made)
                project(1, freed_by=z_made)
            seen.repeat(pe, MH, head_b)

            for r in range(2):
                def outs(i, r=r):
                    for s in range(2):
                        project(s, *((hh, hl) if r == 0 else (yh, yl)), freed_by=x_ready,
                                ready=y_ready if seen.i is None and i == 0 and s == 0 else None)
                seen.repeat(pe, KT // 2, outs)
            for s in range(2):
                seen(raw_full[s], 32 * KT)

        def mlstm_act(act, seen, turn, use):
            def head_a(h):
                seen.back(act, "xmc")
                seen.back(act, "spill")

                def silu(blk):
                    act.wait_ge(*seen(cv_ready))
                    act.activation(xc[:, blk, 0:P], cv[:, blk % 2, 0:P], ACT.Silu, bias=hcol[:, blk:blk + 1])
                    act.activation(xc[:, blk, P:T], cv[:, blk % 2, P + 2:T + 2], ACT.Silu, bias=hcol[:, blk:blk + 1]).then_inc(xc_done, 1)

                for blk in range(MB):
                    b, _ = use(False)
                    act.wait_ge(*seen(proj_done[blk % 2]))
                    act.copy(xm_at(blk, 0, P), acc[b][:, AO:AO + P])
                    act.copy(xm_at(blk, P, T), acc[b][:, AO + P:AO + T]).then_inc(xm_copied, 1)
                    if blk == 0:
                        use(), use()
                    if blk == 1:
                        use()
                    if blk:
                        silu(blk - 1)
                turn()
                silu(MB - 1)
                act.wait_ge(*seen(xc_done, MB))
                seen(xm_copied, MB)
                act.dma_start(scratch["xm"][bass.ds(h, 1)].rearrange("a b p t -> p (a b) t"), xm[:, :, :]).then_inc(spill, 16)
                act.dma_start(scratch["xc"][bass.ds(h, 1)].rearrange("a b p t -> p (a b) t"), xc[:, :, :]).then_inc(spill, 16)
                seen.lend("spill", spill, 32)
                seen.lend("xmc", gates_done)
            seen.repeat(act, MH, head_a)

            act.wait_ge(*seen(g_full))
            for c0, c1, o in GROUPS:
                ins = act.copy(g16[0:16, c0:c1], pt[0:16, o:o + c1 - c0])
            ins.then_inc(g_copied, 1)
            use()
            b, full = use()
            act.wait_ge(*full)
            for c0, c1, o in GROUPS:
                ins = act.activation(r1[:, c0:c1], acc[b][0:64, o:o + c1 - c0], ACT.Abs)
            ins.then_inc(mact_step, 1)
            act.wait_ge(*seen(mact_step))
            act.activation(r1[:, :], r1[:, :], ACT.Exp, scale=-1.0).then_inc(mact_step, 1)
            act.wait_ge(*seen(mact_step))
            act.activation(r1[:, :], r1[:, :], ACT.Ln, bias=ones[0:64, 0:1]).then_inc(ln_ready, 1)
            act.wait_ge(*seen(m_made))
            act.activation(wirow[:, P:T], mrow[:, P:T], ACT.Exp, scale=-1.0, bias=m0[:, 0:1])
            act.activation(wirow[:, 0:P], crow[:, 0:P], ACT.Exp, bias=nml[:, 0:1]).then_inc(rows_ready, 1)
            use()

            def head_b(h):
                for n in range(2):
                    for blk in range(MB):
                        b, full = use()
                        act.wait_ge(*full)
                        if n == 1 and blk == 0:
                            seen.back(act, "y")
                        act.copy((mq, mk)[n][:, blk, :], acc[b][:, AO:AO + T]).then_inc(qkv_copied, 1)
                for u in range(3):
                    b, full = use()
                    act.wait_ge(*full)
                    if u < 2:
                        act.copy(mv[:, 2 * u:2 * u + 2, :], acc[b][:, :].rearrange("p (a c) -> p a c", a=2)).then_inc(qkv_copied, 1)
                    else:
                        act.copy(mv[:, 4, :], acc[b][:, 0:512])
                        act.copy(ktm[:, :], acc[b][:, 512:1024]).then_inc(qkv_copied, 1)
                act.wait_ge(*seen(mdiag_ready, 2))
                for i in range(QT):
                    use()
                    for d in range(2):
                        c0, c1, _ = tri(d, i)
                        t0 = i * P
                        if i:
                            act.wait_ge(*seen(a_made))
                        bias = ccol[:, d, i:i + 1]
                        ins = act.activation(two[:, d, t0:t0 + P], mdg[:, d, t0:t0 + P], ACT.Exp, scale=-1.0, bias=bias)
                        o0, o1 = (t0 + P, c1) if d == 0 else (c0, t0)
                        if i and o1 > o0:
                            src = pt[:, o0 - P:o1 - P] if d == 0 else ob[0][:, o0 - P:o1 - P]
                            ins = act.activation(two[:, d, o0:o1], src, ACT.Exp, scale=-1.0, bias=bias)
                        ins.then_inc(d_full, 1)
                for d in range(2):
                    for n in range(2):
                        b, full = use()
                        act.wait_ge(*full)
                        if d == 1 and n == 0:
                            act.wait_ge(*seen(a_made, 2))
                        if n == 0:
                            ins = act.activation(ht[:, 0, :] if d == 0 else two[:, 0, :], acc[b][:, AO:AO + T], ACT.Exp, scale=-1.0)
                        else:
                            ins = act.copy((ht, two)[d][:, 1, :], acc[b][:, AO:AO + T])
                        ins.then_inc(bc_read, 1)
                for blk in range(MB):
                    ins = act.activation(xm[:, blk, 0:T], xc[:, blk, :], ACT.Copy, scale=hcol[:, 4 + blk:5 + blk])
                ins.then_inc(skip_made, 1)
                for _ in range(4):
                    use(False)

                def state(d):
                    for u in range(2):
                        b, full = use()
                        act.wait_ge(*full)
                        seen.back(act, ("cst", u))
                        act.copy(cst(u), acc[b][:, :].rearrange("p (a c) -> p a c", a=2)).then_inc(cst_copied, 1)
                        act.wait_ge(*seen(cst_copied))
                        act.dma_start(O["mlstm_C"][0, 0, d].rearrange("h (k p) e -> p h k e", p=P)[:, bass.ds(h, 1), 2 * u:2 * u + 2, :]
                                      .rearrange("p a k e -> p (a k) e"), cst(u)).then_inc(c_stored[u], 16)
                        seen.lend(("cst", u), c_stored[u], 16)

                def gate(blk):
                    b, _ = use(False)
                    act.wait_ge(*seen(proj_done[blk % 2]))
                    act.activation(mq[:, blk, :], acc[b][:, AO:AO + T], ACT.Silu).then_inc(z_made, 1)

                state(0)
                use()
                act.wait_ge(*seen(h_sum))
                gate(0)
                gate(1)

                def square(blk):
                    act.activation(two[:, blk % 2, :], mk[:, blk, :], ACT.Square).then_inc(msq_full, 1)

                act.wait_ge(*seen(centred))
                square(0)
                square(1)
                state(1)
                act.wait_ge(*seen(n_full))
                seen.back(act, "nst")
                act.copy(nst(0), ob[0][0:1, :])
                act.copy(nst(1), pt[0:1, 0:MD]).then_inc(n_copied, 1)
                act.wait_ge(*seen(n_copied))
                for d in range(2):
                    act.dma_start(O["mlstm_n"][0, 0, d][bass.ds(h, 1), :], nst(d)).then_inc(n_stored, 16)
                seen.lend("nst", n_stored, 32)
                for blk in (2, 3):
                    act.wait_ge(*seen(msq_used))
                    square(blk)
                seen(msq_used)
                b, full = use()
                act.wait_ge(*full)
                act.activation(rinv[:, :], acc[b][:, AO:AO + T], ACT.Sqrt, bias=eps[:, 0:1], scale=1.0 / MD).then_inc(mroot_ready, 1)
                gate(2)
                gate(3)
                act.wait_ge(*seen(ym_ready))
                act.dma_start(scratch["y"].rearrange("(h b) p t -> p h b t", b=MB)[:, bass.ds(h, 1), :, :].rearrange("p a b t -> p (a b) t"),
                              mk[:, :, :]).then_inc(y_spill, 16)
                seen.lend("y", y_spill, 16)
            seen.repeat(act, MH, head_b)
            for u in range(2):
                seen.back(act, ("cst", u))
            seen.back(act, "nst")
            for d in range(2):
                col = P - 1 if d == 0 else 0
                act.dma_start(O["mlstm_m"][0, 0, d].rearrange("(h a) -> h a", a=1), mnew[32 * d:32 * d + MH, 0:1]).then_inc(m_stored, 16)
            act.wait_ge(m_stored, 32)
            act.copy(flag[:, :], eps[:, 0:1]).then_inc(m_end, 1)
            for r in range(2):
                for kt in range(KT):
                    if kt % MB == 0:
                        act.wait_ge(yb_full[r * 2 + kt // MB], 16)
                    act.copy((hh, yh)[r][:, kt, :], yb[:, r, kt, :]).then_inc(yhi_ready, 1)
            seen(proj_done[0], KT)
            seen(proj_done[1], KT)

        def mlstm_dve(dve, seen, turn, use, step, add_gated):
            def bds(h, n3=3):
                for n in range(3):
                    for blk in range(MB):
                        ins = dve.tensor_tensor(bd[:, n, blk, :].rearrange("p (a c) -> p a c", c=4), headmask.rearrange("p (a c) -> p a c", c=4),
                                                wsm[:, n, head_cols(h, blk), :].to_broadcast([P, 32, 4]), ALU.mult)
                ins.then_inc(bd_ready, 1)

            dve.wait_ge(m_in, 16 * 11)
            for a0, a1 in ((0, 2), (P + 2, P + 4), (T + 4, T + 5)):
                dve.memset(xm[:, :, a0:a1], 0.0)
            dve.memset(wsm[:, :, MI // P:, :], 0.0)
            dve.memset(rones[:, :], 1.0).then_inc(m_ones, 1)
            dve.wait_ge(*seen(m_ones))

            def head_a(h):
                for n in range(MB):
                    ins = dve.tensor_copy(hcol[:, n:n + 1], cols[:, 2, head_cols(h, CONVB + n)])
                    for k in range(4):
                        ins = dve.tensor_copy(hcol[:, 4 + 4 * k + n:5 + 4 * k + n], cols[:, 2, head_cols(h, CONVW + 16 * k + n)])
                step(ins)
                bds(h)
                use(False)
                for n, w in ((0, 8), (8, 4)):
                    b, full = use()
                    dve.wait_ge(*full)
                    dve.tensor_copy(bdt[:, n:n + w, :], acc[b][:, 0:w * P].rearrange("p (a c) -> p a c", c=P)).then_inc(bt_ready, 1)
                for blk in range(MB):
                    if blk:
                        use(False)
                    dve.wait_ge(*seen(xm_copied))
                    if blk == 1:
                        b, full = use()
                        dve.wait_ge(*full)
                        dve.tensor_copy(gm[:, :, :], acc[b][:, 0:128].rearrange("p (a c) -> p a c", c=32)).then_inc(gm_ready, 1)
                    seen.back(dve, ("cv", blk % 2))
                    W = T + 2
                    step(dve.tensor_scalar(cv[:, blk % 2, 0:W], xm[:, blk, 0:W], hcol[:, 4 + blk:5 + blk], None, ALU.mult))
                    for k in range(1, 4):
                        ins = dve.scalar_tensor_tensor(out=cv[:, blk % 2, 0:W], in0=xm[:, blk, k:k + W],
                                                       scalar=hcol[:, 4 + 4 * k + blk:5 + 4 * k + blk], in1=cv[:, blk % 2, 0:W],
                                                       op0=ALU.mult, op1=ALU.add)
                        if k < 3:
                            step(ins)
                    ins.then_inc(cv_ready, 1)
                    seen.lend(("cv", blk % 2), xc_done)
                turn()
                dve.wait_ge(*seen(cv_ready, MB))
                seen.back(dve, ("cv", 1))
            seen.repeat(dve, MH, head_a)

            b, full = use()
            dve.wait_ge(*full)
            for c0, c1, o in GROUPS:
                ins = dve.tensor_copy(crow[:, c0:c1], acc[b][0:64, o:o + c1 - c0])
            ins.then_inc(row_read, 1)
            b, full = use()
            dve.wait_ge(*seen(ln_ready))
            for c0, c1, o in GROUPS:
                ins = dve.scalar_tensor_tensor(out=r2[:, c0:c1], in0=acc[b][0:64, o:o + c1 - c0], scalar=0.0, in1=r1[:, c0:c1],
                                               op0=ALU.min, op1=ALU.subtract)
            ins.then_inc(row_read, 1)
            dve.wait_ge(*seen(row_read, 2))
            segs = [(0, slice(0, P), slice(0, P)), (0, slice(P, T), slice(P, T)),
                    (32, slice(0, P), slice(P - 1, None, -1)), (32, slice(P, T), slice(T - 1, P - 1, -1))]
            for p0, _, c in segs:
                ins = dve.tensor_tensor_scan(out=bmrow[p0:p0 + 32, c], data0=rones[p0:p0 + 32, c], data1=r2[p0:p0 + 32, c],
                                             initial=0.0, op0=ALU.mult, op1=ALU.add)
            step(ins)
            step(dve.tensor_tensor(crow[:, :], crow[:, :], bmrow[:, :], ALU.subtract))
            for p0, f, c in segs:
                ins = dve.tensor_tensor_scan(out=mrow[p0:p0 + 32, c], data0=crow[p0:p0 + 32, c], data1=crow[p0:p0 + 32, c],
                                             initial=0.0 if f.start == 0 else m0[p0:p0 + 32, 0:1], op0=ALU.max, op1=ALU.max)
            step(ins)
            for d, col in ((0, P - 1), (1, 0)):
                ins = dve.tensor_scalar(nml[32 * d:32 * d + 32, :], mrow[32 * d:32 * d + 32, col:col + 1], -1.0, None, ALU.mult)
            step(dve.tensor_tensor(bmrow[:, :], bmrow[:, :], mrow[:, :], ALU.add))
            for d, col in ((0, P - 1), (1, 0)):
                ins = dve.tensor_copy(mnew[32 * d:32 * d + 32, :], bmrow[32 * d:32 * d + 32, col:col + 1])
            ins.then_inc(m_made, 1)
            b, full = use()
            dve.wait_ge(*full)
            dve.tensor_copy(nall[:, :, :], acc[b][:, 384:416].rearrange("p (d c) -> p d c", d=2))
            dve.tensor_copy(ct[:, :, :], acc[b][:, 0:384].rearrange("p (a c) -> p a c", c=64)).then_inc(row_read, 1)
            dve.wait_ge(*seen(row_read))

            def prepare(h):
                for d in range(2):
                    row = slice(h + 32 * d, h + 32 * d + 1) if isinstance(h, int) else bass.ds(h + 32 * d, 1)
                    dve.tensor_copy(sel[:, d, :], ident[0:64, row].to_broadcast([64, P]))
                    dve.tensor_copy(ccol[:, d, :], ct[:, :, row].rearrange("p a b -> p (a b)"))
                bds(h)

            def head_b(h):
                for n in range(MB):
                    dve.tensor_copy(hcol[:, n:n + 1], cols[:, 2, head_cols(h, MHG + n)])
                    ins = dve.tensor_copy(hcol[:, 4 + n:5 + n], cols[:, 2, head_cols(h, SKIP + n)])
                step(ins)
                for _ in range(11):
                    use()
                dve.wait_ge(*seen(mb_full, 2))
                for d in range(2):
                    mask = mc[:, (2 + d) * P:(3 + d) * P]
                    src = (pt[:, 0:512], pt[:, 512:640]) if d == 0 else (ob[0][:, :], ob[1][:, 0:P])
                    for u in range(4):
                        dve.tensor_tensor(mdg[:, d, P + u * P:P + (u + 1) * P], src[0][:, u * P:(u + 1) * P], mask, ALU.add)
                    dve.tensor_tensor(mdg[:, d, 0:P], src[1], mask, ALU.add).then_inc(mdiag_ready, 1)
                for i in range(QT):
                    b, full = use()
                    dve.wait_ge(*full)
                    for d in range(2):
                        c0, c1, o = tri(d, i)
                        dve.wait_ge(*seen(d_full))
                        s0 = c0 if i == 0 else c0 - P
                        dve.scalar_tensor_tensor(out=amat[:, d * AW + o:d * AW + o + c1 - c0], in0=acc[b][:, s0:s0 + c1 - c0],
                                                 scalar=MD ** -0.5, in1=two[:, d, c0:c1], op0=ALU.mult, op1=ALU.mult).then_inc(a_made, 1)
                for _ in range(4):
                    use()
                for d in range(2):
                    em, wi = (ht, two)[d][:, 0, :], (ht, two)[d][:, 1, P:T]
                    for kt in range(4):
                        ins = dve.tensor_copy(nrep[:, kt, :], nall[:, d, head_cols(h, kt)].to_broadcast([P, P]))
                    dve.wait_ge(*seen(bc_read, 2))
                    for kt in range(4):
                        seen.back(dve, ("qw", kt % 2))
                        dve.tensor_tensor(mdg[:, kt % 2, 0:NS], mq[:, kt, P:T], wi, ALU.mult).then_inc(qw_full, 1)
                        seen.lend(("qw", kt % 2), c_used[kt % 2])
                    bb = [use(False)[0], use(False)[0]]
                    dve.wait_ge(*seen(den_full))
                    for src, c0, c1 in ((ob[0][:, :], P, T), (ob[1][:, 0:P], 0, P)):
                        step(dve.tensor_tensor(em[:, c0:c1], src, em[:, c0:c1], ALU.max))
                        ins = dve.scalar_tensor_tensor(out=em[:, c0:c1], in0=src, scalar=-1.0, in1=em[:, c0:c1], op0=ALU.mult, op1=ALU.max)
                    ins.then_inc(den_read, 1)
                    dve.wait_ge(*seen(den_read))
                    step(dve.reciprocal(em, em))
                    seen.back(dve, ("qw", 1))
                    out = mk if d == 0 else mq
                    for e in range(4):
                        dve.tensor_tensor(out[:, e, P:T], acc[bb[e // 2]][:, (e % 2) * 512:(e % 2) * 512 + 512], em[:, P:T], ALU.mult)
                        ins = dve.tensor_tensor(out[:, e, 0:P], pt[:, 512 + e * P:512 + (e + 1) * P], em[:, 0:P], ALU.mult)
                    ins.then_inc(h_done, 1)
                    dve.wait_ge(*seen(h_done))
                    if d == 0:
                        for n in range(2):
                            dve.tensor_scalar(ht[:, n, 0:MD], ktm[:, :], ccol[:, n, 5:6], MD ** -0.5, ALU.mult, ALU.mult).then_inc(kw_ready, 1)
                        dve.wait_ge(*seen(kw_ready, 2))
                        prepare(h + 1)
                dve.tensor_tensor(mk[:, :, :], mk[:, :, :], mq[:, :, :], ALU.add).then_inc(h_sum, 1)
                use(), use()
                b, full = use()
                dve.wait_ge(*full)
                dve.wait_ge(*seen(h_sum))
                for blk in range(MB):
                    ins = dve.scalar_tensor_tensor(out=mk[:, blk, :], in0=acc[b][:, AO:AO + T], scalar=-1.0 / MD, in1=mk[:, blk, :],
                                                   op0=ALU.mult, op1=ALU.add)
                ins.then_inc(centred, 1)
                use(False), use(False)
                use(), use()
                use()
                use(False), use(False)
                dve.wait_ge(*seen(centred))
                dve.wait_ge(*seen(mroot_ready))
                step(dve.reciprocal(rinv[:, :], rinv[:, :]))
                for blk in range(MB):
                    ins = dve.tensor_tensor(mk[:, blk, :], mk[:, blk, :], rinv[:, :], ALU.mult)
                step(ins)
                for blk in range(MB):
                    ins = dve.scalar_tensor_tensor(out=mk[:, blk, :], in0=mk[:, blk, :], scalar=hcol[:, blk:blk + 1], in1=xm[:, blk, 0:T],
                                                   op0=ALU.mult, op1=ALU.add)
                ins.then_inc(skip_added, 1)
                dve.wait_ge(*seen(skip_added))
                dve.wait_ge(*seen(z_made, 4))
                for stored in (*c_stored, n_stored):
                    dve.wait_ge(*seen(stored, 32))
                dve.tensor_tensor(mk[:, :, :], mk[:, :, :], mq[:, :, :], ALU.mult).then_inc(ym_ready, 1)
            prepare(0)
            seen.repeat(dve, MH, head_b)
            for s in range(2):
                seen(proj_done[s], 4 * MH)
            for r in range(2):
                for kt in range(KT):
                    dve.wait_ge(*seen(yhi_ready))
                    dve.tensor_tensor((hl, yl)[r][:, kt, :], yb[:, r, kt, :], (hh, yh)[r][:, kt, :].bitcast(F32), ALU.subtract).then_inc(y_ready, 1)
            for r in range(2):
                def outs(i, r=r):
                    for s in range(2):
                        add_gated(s, i * 2 + s)
                seen.repeat(dve, KT // 2, outs)
                dve.wait_ge(*seen(x_ready, KT))

        block = ctx.enter_context(nc.Block())

        @block.sync
        def _(sp):
            seen = Seen()

            def panel(slot, parts, reader):
                seen.back(sp, ("raw", slot))
                for dst, src in parts:
                    sp.dma_start(dst, src).then_inc(raw_full[slot], 16)
                seen.lend(("raw", slot), reader[slot])

            def whole(slot, w, c, reader=w_full):
                v = w_at(w, c)
                panel(slot, [(raw[:, slot, 0:4, :], v[:, 0:4, :]), (raw[:, slot, 4:8, :], v[:, 4:8, :])], reader)

            c4 = A["consts"]
            sp.dma_start(consts[:, :, :], c4[:, 0:4 * P].rearrange("p (a c) -> p a c", a=4)).then_inc(const_in, 16)
            sp.dma_start(cs[:, :, :], c4[:, 4 * P:4 * P + 2 * NS].rearrange("p (a c) -> p a c", a=2)).then_inc(const_in, 16)
            for i, n in enumerate(("q1", "k1", "q2", "k2")):
                sp.dma_start(lamr[0:1, i, :], A["diff_lambda_" + n]).then_inc(const_in, 16)
            for dst, src in row_parts(rows, A):
                sp.dma_start(dst, src).then_inc(rows_in, 16)
            def load_x():
                for t in range(QT):
                    src = A["x_prompt"][0] if t == 0 else A["x_sample"][0, (t - 1) * P:t * P, :]
                    seen.back(sp, ("xin", t % 2))
                    sp.dma_start(xtile[t % 2], src.rearrange("p (a c) -> p a c", a=2)).then_inc(xin_full[t % 2], 16)
                    seen.lend(("xin", t % 2), acc_full[t % 2])

            def mod_panel(layer, slot, c):
                if layer < DEPTH:
                    whole(slot, A["w_mod"][layer], c, raw_used)

            def mod_turn(i):
                for s in range(6):
                    if s == RAW and seen.i is None:
                        load_x()
                    mod_panel(0, s % RAW, i * (6 * P) + s * P)
            seen.repeat(sp, 4, mod_turn)

            for layer, kind in enumerate(kinds):
                j = layer // 3
                if kind == "gqa":
                    w = A["gqa_w_in"][j]
                    ckd, cvd = (A[f"cache_gqa_{n}"][0, j].rearrange("t h d -> t (h d)") for n in "kv")

                    def group(g):
                        panel(2, [(raw[:, 2, :, 0:HD], w_at(w, g * HD + GQ_Q * HD, HD)),
                                  (raw[:, 2, :, HD:P], w_at(w, g * HD + (GQ_Q + GQ_KV) * HD, HD))], w_full)
                        whole(0, w, g * (2 * P))
                        whole(1, w, g * (2 * P) + P)
                        whole(0, w, g * (2 * P) + (GQ_Q + 2 * GQ_KV) * HD)
                        if layer and seen.i is None:
                            sp.wait_ge(x_ready, sum(XR[:layer]))
                        seen.back(sp, "ck")
                        whole(1, w, g * (2 * P) + (GQ_Q + 2 * GQ_KV) * HD + P)
                        sp.dma_start(ck[:, 0:HD], ckd[:, bass.ds(g * HD, HD)]).then_inc(cache_full, 16)
                        sp.dma_start(ck[:, HD:P], cvd[:, bass.ds(g * HD, HD)]).then_inc(cache_full, 16)
                        seen.lend("ck", v_used)
                        for s in range(6):
                            mod_panel(layer + 1, (2, 0, 1)[s % 3], g * (6 * P) + s * P)
                    seen.repeat(sp, GQ_KV, group)
                    wo = A["gqa_w_out"][j]
                elif kind == "diff":
                    w = A["diff_w_in"][0]
                    ckd = A["cache_diff_k"][0, 0].rearrange("t h a d -> t (h a d)")
                    cvd = A["cache_diff_v"][0, 0].rearrange("t h d -> t (h d)")

                    def head(n):
                        for s, c in enumerate((0, D, 2 * D, 3 * D)):
                            if s == 3:
                                seen.back(sp, "ck")
                            whole(s % 2, w, n * P + c)
                        sp.dma_start(ck[:, :], ckd[:, bass.ds(n * P, P)]).then_inc(cache_full, 16)
                        sp.dma_start(vtm[:, QT, :], cvd[:, bass.ds(n * P, P)]).then_inc(vc_full, 16)
                        seen.lend("ck", v_used)
                        for s in range(3):
                            mod_panel(layer + 1, 2, n * (3 * P) + s * P)
                    seen.repeat(sp, KT, head)
                    wo = A["diff_w_out"][0]
                else:
                    mlstm_sp(sp, seen, whole, mod_panel)
                    continue

                def outs(i):
                    for s in range(2):
                        whole(s, wo, i * (2 * P) + s * P)
                seen.repeat(sp, KT // 2, outs)

        @block.gpsimd
        def _(pool):
            seen = Seen()
            pool.memset(eps[:, 0:1], EPS)
            pool.memset(eps[:, 1:2], EPS / SM ** 2).then_inc(eps_set, 1)

            def split(s):
                pool.wait_ge(*seen(raw_full[s], 32))
                seen.back(pool, ("w", s))
                pool.tensor_tensor(idle[:, :], eps[:, 0:1], eps[:, 0:1], ALU.add)
                pool.tensor_copy(wh[:, s], raw[:, s]).then_inc(pool_step, 1)
                pool.wait_ge(*seen(pool_step))
                pool.tensor_tensor(wl[:, s], raw[:, s], wh[:, s].bitcast(F32), ALU.subtract).then_inc(w_full[s], 1)
                seen.lend(("w", s), proj_done[s])

            def mod_panels(layer, counts):
                for s, n in enumerate(counts):
                    if layer < DEPTH:
                        seen(raw_full[s], 32 * n)

            mod_panels(0, MODS[None][0])
            for layer, kind in enumerate(kinds):
                if kind == "mlstm":
                    mlstm_pool(pool, seen, split, mod_panels)
                    continue

                def panels(order, mods=()):
                    def turn(i):
                        for s in order:
                            split(s)
                        mod_panels(layer + 1, mods)
                    return turn
                seen.repeat(pool, *((GQ_KV, panels((2, 0, 1, 0, 1), (2, 2, 2))) if kind == "gqa" else
                                    (KT, panels((0, 1, 0, 1), (0, 0, 3)))))
                seen.repeat(pool, KT // 2, panels((0, 1)))

        @block.tensor
        def _(pe):
            seen, turn = Seen(), Turns()

            def buffer(freed_by=acc_free):
                b = turn()
                seen.back(pe, ("acc", b))
                if freed_by is None:
                    seen.marks.pop(("acc", b), None)
                else:
                    seen.lend(("acc", b), freed_by[b] if freed_by is acc_free else freed_by)
                return b

            def project(s, hi=hh, lo=hl, ready=None, freed_by=acc_free):
                b = buffer(freed_by)
                pe.wait_ge(*seen(w_full[s]))
                for kt in range(KT):
                    if ready is not None:
                        pe.wait_ge(*seen(ready))
                    for n, (w, h) in enumerate(((wh, hi), (wh, lo), (wl, hi))):
                        for t, c in halves():
                            ins = pe.matmul(acc[b][:, c:c + 320], w[:, s, kt, :], h[:, kt, t:t + 320],
                                            start=kt == 0 and n == 0, stop=kt == KT - 1 and n == 2)
                ins.then_inc(proj_done[s], 1)

            def wide(lhsT, rhs, start=True, stop=True, b=None, parts=P):
                for t, c in halves():
                    ins = pe.matmul(acc[b][0:parts, c:c + 320], lhsT, rhs[:, t:t + 320], start=start, stop=stop)
                return ins

            def sum_squares():
                b = buffer(root_ready)
                for kt in range(KT):
                    pe.wait_ge(*seen(sq_full))
                    ins = wide(ones, two[:, kt % 2, :], kt == 0, kt == KT - 1, b)
                    ins.then_inc(sq_used if kt < KT - 1 else acc_full[b], 1)

            def mod_panel(layer, slot, n):
                if layer < DEPTH:
                    pe.wait_ge(*seen(raw_full[slot], 32))
                    for kt in range(KT):
                        ins = pe.matmul(ob[1][:, bass.ds(2 * n + MO, 2)], raw[:, slot, kt, :], cond[:, kt:2 * KT:KT],
                                        start=kt == 0, stop=kt == KT - 1, skip_group_check=True)
                    ins.then_inc(raw_used[slot], 1)

            def pool_takes(*counts):
                for s, n in enumerate(counts):
                    seen(raw_full[s], 32 * n)

            pe.wait_ge(const_in, 16 * 6)
            pe.wait_ge(rows_in, 16 * len(row_parts(rows, A)))
            for i, n in enumerate((P, 29, 112)):
                ins = pe.transpose(pt[:, i * P:i * P + n], rows[0:n, i, :], ident[0:n, 0:n])
            ins.then_inc(cols_turned, 1)
            for t in range(QT):
                b = buffer(x_in)
                pe.wait_ge(*seen(xin_full[t % 2], 16))
                for kt in range(KT):
                    ins = pe.transpose(acc[b][:, kt * P:(kt + 1) * P], xtile[t % 2][:, kt // 4, (kt % 4) * P:(kt % 4 + 1) * P], ident)
                ins.then_inc(acc_full[b], 1)
            pe.wait_ge(*seen(lam_ready))
            pe.matmul(ob[0][:, 0:1], ones[0:1, :], lamt[0:1, 4:5], start=True, stop=True).then_inc(lam_sent, 1)
            seen.lend("ob0", cols_ready)
            pe.wait_ge(*seen(cond_ready))

            def scores(k, qs, m):
                qt, _ = steps[k]
                b = buffer(None)
                q = qst[:, qs, qt * P:(qt + 1) * P]
                for c0, c1, o in ([(0, P, AO)] if qt == 0 else [(P, P + 320, AO), (P + 320, P + 640, AO + 320)]):
                    for n in range(2):
                        ins = pe.matmul(acc[b][:, o:o + c1 - c0], q, kst[:, m, n, c0:c1], start=n == 0, stop=n == 1)
                ins.then_inc(acc_full[b], 1)

            def turn_p(src, qt):
                for i in range(1 if qt == 0 else 5):
                    ins = pe.transpose(pt[:, TO + i * P:TO + (i + 1) * P], src[:, i * P:(i + 1) * P], ident)
                ins.then_inc(pt_full, 1)

            def copied(qt):
                pe.wait_ge(*seen(pts_dve))
                if qt > 0:
                    pe.wait_ge(*seen(pts_act))

            def values(slot, qt, vals, last=None):
                seen.back(pe, f"ob{slot}")
                n = 1 if qt == 0 else 5
                for i in range(n):
                    ins = pe.matmul(ob[slot][:, 0:vals(0).shape[-1]], ht[:, slot, i * P:(i + 1) * P],
                                    vals(i if qt == 0 else i + 1), start=i == 0, stop=i == n - 1)
                ins.then_inc(ob_full[slot], 1)
                seen.lend(f"ob{slot}", last or ob_free[slot])

            def turn_out(end):
                b = buffer(yt_ready)
                for t in range(QT):
                    ins = pe.transpose(acc[b][:, TO + t * P:TO + (t + 1) * P], osb[:, t, :], ident)
                    if end and t == 0:
                        ins.then_inc(v_used, 1)
                ins.then_inc(acc_full[b], 1)

            def rotate(src):
                b = buffer(rot_read)
                pe.matmul(acc[b][:, 0:NS], perm, src[:, P:T], start=True, stop=True).then_inc(acc_full[b], 1)

            def head_sums(slot):
                b = buffer(nroot_ready)
                pe.wait_ge(*seen(sq_full))
                wide(half1, two[:, slot, :], b=b).then_inc(acc_full[b], 1)

            def gqa_group(g, layer):
                first = seen.i is None
                pool_takes(2, 2, 1)
                project(2, ready=h_ready if first else None)
                project(0)
                head_sums(0)
                project(1)
                head_sums(1)
                head_sums(0)
                project(0)
                for src in (kv, qn[:, 0], qn[:, 1]):
                    pe.wait_ge(*seen(qk_scaled))
                    rotate(src)
                b = buffer(tm_ready)
                for t in range(QT):
                    pe.transpose(acc[b][:, TO + t * P:TO + (t + 1) * P], kv[:, t * P:(t + 1) * P], ident)
                pe.wait_ge(*seen(cache_full, 32))
                pe.transpose(acc[b][:, TO + T:TO + T + P], ck[:, :], ident).then_inc(acc_full[b], 1)
                project(1)
                pe.wait_ge(*seen(st_ready))

                def outputs(k):
                    values(k % 2, steps[k][0], lambda t: vtm[:, t, HD:P] if t < QT else ck[:, HD:P])

                for blk in range(2):
                    scores(0, 2 * blk, 0)
                    scores(1, 2 * blk + 1, 0)
                    for k in range(NST):
                        pe.wait_ge(*seen(p_ready))
                        if k + 2 < NST:
                            scores(k + 2, 2 * blk + k % 2, 0)
                        if k:
                            copied(steps[k - 1][0])
                        turn_p(two[:, k % 2], steps[k][0])
                        if k in (2, 6, 8):
                            m = 3 * blk + (k - 1) // 3
                            seen.back(pe, "ob1")
                            mod_panel(layer + 1, (2, 0, 1)[m % 3], g * 6 + m)
                        if k:
                            outputs(k - 1)
                    copied(steps[-1][0])
                    outputs(NST - 1)
                    for o in range(2):
                        seen.back(pe, f"ob{o}")
                    turn_out(blk == 1)

            def diff_head(n, layer):
                first = seen.i is None
                pool_takes(2, 2)
                for name, s in (("q", 0), ("k", 1), ("v", 0)):
                    project(s, ready=h_ready if first and name == "q" else None, freed_by=raw_copied)
                    seen.marks[name] = seen.marks[("acc", (turn.k - 1) % 2)]
                for name, src in (("q", qn[:, 0]), ("k", kv)):
                    seen.back(pe, name)
                    rotate(src)
                b = buffer(tm_ready)
                seen.back(pe, "v")
                for t in range(QT):
                    ins = pe.transpose(acc[b][:, TO + t * P:TO + (t + 1) * P], qn[:, 1, t * P:(t + 1) * P], ident)
                ins.then_inc(acc_full[b], 1)
                b = buffer(tm_ready)
                pe.transpose(acc[b][:, 0:P], kv[:, 0:P], ident).then_inc(acc_full[b], 1)
                b = buffer(tm_ready)
                pe.wait_ge(*seen(cache_full, 16))
                pe.transpose(acc[b][:, 0:P], ck[:, :], ident).then_inc(acc_full[b], 1)
                project(1)
                pe.wait_ge(*seen(st_ready))
                pe.wait_ge(*seen(vc_full, 16))

                def outputs(qt):
                    copied(qt)
                    if qt in (1, 3):
                        seen.back(pe, "ob1")
                        mod_panel(layer + 1, 2, n * 3 + qt // 2)
                    values(qt % 2, qt, lambda t: vtm[:, t, :], osb_ready if qt == QT - 1 else None)

                scores(0, 0, 0)
                scores(1, 1, 1)
                for qt in range(QT):
                    pe.wait_ge(*seen(e_ready, 2))
                    if qt + 1 < QT:
                        scores(2 * qt + 2, 0, 0)
                        scores(2 * qt + 3, 1, 1)
                    if qt:
                        outputs(qt - 1)
                    pe.wait_ge(*seen(comb_ready))
                    turn_p(comb, qt)
                outputs(QT - 1)
                seen.back(pe, "ob1")
                mod_panel(layer + 1, 2, n * 3 + 2)
                pe.wait_ge(*seen(o_scaled))
                turn_out(True)

            def mod_turn(i):
                for s in range(6):
                    mod_panel(0, s % RAW, i * 6 + s)
            seen.repeat(pe, 4, mod_turn)

            for layer, kind in enumerate(kinds):
                sum_squares()
                if kind == "mlstm":
                    mlstm_pe(pe, seen, turn, buffer, project, mod_panel, pool_takes)
                    continue
                seen.repeat(pe, *((GQ_KV, lambda g: gqa_group(g, layer)) if kind == "gqa" else
                                  (KT, lambda n: diff_head(n, layer))))
                pe.wait_ge(*seen(y_ready, KT))

                def outs(i):
                    for s in range(2):
                        project(s, yh, yl, freed_by=x_ready)
                seen.repeat(pe, KT // 2, outs)
                pool_takes(KT // 2, KT // 2)
            sum_squares()
            pe.wait_ge(*seen(normed))
            for t in range(QT):
                b = buffer(out_ready)
                for kt in range(KT):
                    ins = pe.transpose(acc[b][:, kt * P:(kt + 1) * P], x[:, kt, t * P:(t + 1) * P], ident)
                ins.then_inc(acc_full[b], 1)

        @block.scalar
        def _(act):
            seen, turn = Seen(), Turns()

            def use(full=True):
                b = turn()
                return (b, seen(acc_full[b])) if full else (b, None)

            def wide(b, rows=P):
                return acc[b][0:rows, AO:AO + T]

            act.wait_ge(eps_set, 1)
            act.wait_ge(*seen(cols_ready))
            act.activation(cond[:, :], cols[:, 1, 0:16], ACT.Silu).then_inc(cond_ready, 1)
            act.wait_ge(*seen(lam_sum))
            act.activation(lamt[0:1, 2:4], lamt[0:1, 0:2], ACT.Exp).then_inc(lam_exp, 1)
            for t in range(QT):
                b, full = use()
                act.wait_ge(*full)
                act.copy(x[:, :, t * P:(t + 1) * P], acc[b][:, :].rearrange("p (k c) -> p k c", c=P)).then_inc(x_in, 1)

            def norm_squares():
                for kt in range(KT):
                    if kt >= 2:
                        act.wait_ge(*seen(sq_used))
                    act.activation(two[:, kt % 2, :], x[:, kt, :], ACT.Square).then_inc(sq_full, 1)
                seen(sq_used)
                b, full = use()
                act.wait_ge(*full)
                act.activation(rinv[:, :], wide(b), ACT.Sqrt, bias=eps[:, 0:1], scale=1.0 / D).then_inc(root_ready, 1)

            def modulate():
                act.wait_ge(*seen(mod_ready))
                for kt in range(KT):
                    s = kt % 2
                    act.wait_ge(*seen(xr_full))
                    if kt >= 2:
                        act.wait_ge(*seen(h_ready))
                    act.activation(ht[:, s, 0:P], two[:, s, 0:P], ACT.Identity, bias=mod[:, kt, 0:1], scale=amul[:, kt, 0:1])
                    act.activation(ht[:, s, P:T], two[:, s, P:T], ACT.Identity, bias=mod[:, kt, 1:2], scale=amul[:, kt, 1:2]).then_inc(xr_used, 1)
                    act.wait_ge(*seen(xr_used))
                    act.copy(hh[:, kt, :], ht[:, s, :]).then_inc(ht_full, 1)
                seen(h_ready, 2)

            def numerators(k, w, ready=p_ready, into=two):
                b, full = use()
                act.wait_ge(*seen(nb_ready))
                act.activation(into[:, k % 2, 0:w], acc[b][:, AO:AO + w], ACT.Exp, bias=st[:, k % 4, 1:2], scale=1.0,
                               accum_out=st[:, k % 4, 2:3]).then_inc(ready, 1)

            def turned(slot, qt):
                act.wait_ge(*seen(pt_full))
                if qt > 0:
                    act.copy(ht[:, slot, BM:T], pt[:, TO + BM:TO + T]).then_inc(pts_act, 1)

            def y_high(n):
                act.wait_ge(*seen(yt_ready))
                act.copy(yh[:, n:n + 1, :] if isinstance(n, int) else yh[:, bass.ds(n, 1), :],
                         comb[:, :].rearrange("p (a t) -> p a t", a=1)).then_inc(yhi_ready, 1)

            width = lambda qt: P if qt == 0 else T

            def gqa_group(g, j=0):
                def squares(s, slot, dst):
                    b, _ = use(False)
                    act.wait_ge(*seen(proj_done[s]))
                    act.activation(two[:, slot, :], wide(b), ACT.Square).then_inc(sq_full, 1)
                    act.copy(dst, wide(b)).then_inc(acc_free[b], 1)

                def root(slot, n, by=0):
                    b, full = use()
                    act.wait_ge(*full)
                    act.activation(ht[0:n, slot, :], wide(b, n), ACT.Sqrt, bias=eps[0:n, by:by + 1],
                                   scale=1.0 / HD / (SM ** 2 if by else 1)).then_inc(nroot_ready, 1)

                def gate(s):
                    b, _ = use(False)
                    act.wait_ge(*seen(proj_done[s]))
                    act.activation(z[:, s, :], wide(b), ACT.Silu).then_inc(acc_free[b], 1)

                squares(2, 0, kv[:, 0:T])
                squares(0, 1, qn[:, 0, :])
                root(0, HD)
                squares(1, 0, qn[:, 1, :])
                root(1, P, 1)
                act.wait_ge(*seen(qk_scaled))
                root(0, P, 1)
                gate(0)
                for _ in range(3):
                    use()
                b, full = use()
                act.wait_ge(*full)
                seen.back(act, "vtm0")
                seen.back(act, "kp")
                act.copy(vtm[:, 0:QT, HD:P], acc[b][:, TO:TO + T].rearrange("p (a c) -> p a c", a=QT)[:, :, HD:P])
                act.copy(kp[:, 0:HD], acc[b][:, TO:TO + HD])
                act.copy(kv[0:HD, T:T + PAST], acc[b][0:HD, TO + T:TO + T + P]).then_inc(tm_ready, 1)
                act.wait_ge(*seen(tm_ready))
                act.dma_start(O["gqa_k"][0, j].rearrange("t h d -> t (h d)")[:, bass.ds(g * HD, HD)], kp[:, 0:HD]).then_inc(store_k, 16)
                act.dma_start(O["gqa_v"][0, j].rearrange("t h d -> t (h d)")[:, bass.ds(g * HD, HD)], vtm[:, 0, HD:P]).then_inc(store_v, 16)
                seen.lend("kp", store_k, 16)
                seen.lend("vtm0", store_v, 16)
                act.wait_ge(*seen(qk_turned))
                act.copy(kst[0:HD, 0, 0, :], kv[0:HD, :])
                act.copy(kst[HD:P, 0, 0, :], kv[0:HD, :]).then_inc(hi_ready, 1)
                seen(qk_scaled, 2)
                for blk in range(2):
                    act.wait_ge(*seen(qk_turned))
                    act.copy(qst[0:HD, 2 * blk, :], qn[0:HD, blk, :])
                    act.copy(qst[HD:P, 2 * blk + 1, :], qn[HD:P, blk, :]).then_inc(hi_ready, 1)
                gate(1)
                for blk in range(2):
                    numerators(0, P)
                    numerators(1, P)
                    for k in range(NST):
                        turned(k % 2, steps[k][0])
                        if k + 2 < NST:
                            numerators(k + 2, width(steps[k + 2][0]))
                    use()
                    y_high(g * 2 + blk)

            def diff_head(n):
                q = qn[:, 0, :]
                for s, dst in ((0, q), (1, kv[:, 0:T]), (0, qn[:, 1, :])):
                    b, _ = use(False)
                    act.wait_ge(*seen(proj_done[s]))
                    act.activation(dst, wide(b), ACT.Copy, scale=SM if dst is q else 1.0).then_inc(raw_copied, 1)
                use(), use()
                b, full = use()
                act.wait_ge(*full)
                seen.back(act, "vtm0")
                act.copy(vtm[:, 0:QT, :], acc[b][:, TO:TO + T].rearrange("p (a c) -> p a c", a=QT)).then_inc(tm_ready, 1)
                b, full = use()
                act.wait_ge(*full)
                seen.back(act, "kp")
                act.copy(kp[:, :], acc[b][:, 0:P]).then_inc(tm_ready, 1)
                b, full = use()
                act.wait_ge(*full)
                act.copy(kv[:, T:T + PAST], acc[b][:, 0:P]).then_inc(tm_ready, 1)
                act.wait_ge(*seen(tm_ready, 3))
                act.dma_start(O["diff_k"][0, 0].rearrange("t h a d -> t (h a d)")[:, bass.ds(n * P, P)], kp[:, :]).then_inc(store_k, 16)
                act.dma_start(O["diff_v"][0, 0].rearrange("t h d -> t (h d)")[:, bass.ds(n * P, P)], vtm[:, 0, :]).then_inc(store_v, 16)
                seen.lend("kp", store_k, 16)
                seen.lend("vtm0", store_v, 16)
                act.wait_ge(*seen(qk_turned))
                act.copy(qst[0:HD, 0, :], qn[0:HD, 0, :])
                act.copy(qst[HD:P, 1, :], qn[HD:P, 0, :]).then_inc(hi_ready, 1)
                act.wait_ge(*seen(qk_turned))
                for m in range(2):
                    act.copy(kst[0:HD, m, 0, :], kv[HD * m:HD * m + HD, :])
                    ins = act.copy(kst[HD:P, m, 0, :], kv[HD * m:HD * m + HD, :])
                ins.then_inc(hi_ready, 1)
                b, _ = use(False)
                act.wait_ge(*seen(proj_done[1]))
                act.activation(z[:, 0, :], wide(b), ACT.Silu).then_inc(acc_free[b], 1)
                numerators(0, P, e_ready)
                numerators(1, P, e_ready)
                for qt in range(QT):
                    if qt:
                        turned((qt - 1) % 2, qt - 1)
                    if qt + 1 < QT:
                        for m in range(2):
                            numerators(2 * qt + 2 + m, T, e_ready, (two, qn)[(qt + 1) % 2])
                turned((QT - 1) % 2, QT - 1)
                act.wait_ge(*seen(osb_ready))
                for t in range(QT):
                    ins = act.activation(two[:, 0, t * P:(t + 1) * P], osb[:, t, :], ACT.Square, accum_out=oss[:, t:t + 1])
                ins.then_inc(act_step, 1)
                act.wait_ge(*seen(act_step))
                act.activation(oss[:, 0:QT], oss[:, 0:QT], ACT.Sqrt, bias=eps[:, 0:1], scale=1.0 / P).then_inc(oroot_ready, 1)
                use()
                y_high(n)

            act.wait_ge(*seen(x_in, QT))
            for layer, kind in enumerate(kinds):
                if layer:
                    act.wait_ge(*seen(x_ready, XR[layer - 1]))
                if kind == "mlstm":
                    seen.back(act, "vtm0")
                    seen.back(act, "kp")
                    act.copy(flag[:, :], eps[:, 0:1]).then_inc(m_begin, 1)
                norm_squares()
                modulate()
                if kind == "mlstm":
                    mlstm_act(act, seen, turn, use)
                    continue
                seen.repeat(act, *((GQ_KV, lambda g: gqa_group(g, layer // 3)) if kind == "gqa" else (KT, diff_head)))
                seen(proj_done[0], KT // 2)
                seen(proj_done[1], KT // 2)
            act.wait_ge(*seen(x_ready, XR[-1]))
            norm_squares()
            for t in range(QT):
                b, full = use()
                act.wait_ge(*full)
                seen.back(act, ("y", t % 2))
                act.copy(xtile[t % 2], acc[b][:, :].rearrange("p (a c) -> p a c", a=2)).then_inc(out_ready, 1)
                act.wait_ge(*seen(out_ready))
                dst = O["y_prompt"][0] if t == 0 else O["y_sample"][0, (t - 1) * P:t * P, :]
                act.dma_start(dst.rearrange("p (a c) -> p a c", a=2), xtile[t % 2]).then_inc(y_stored[t % 2], 16)
                seen.lend(("y", t % 2), y_stored[t % 2], 16)
            for stored in (store_k, store_v, *y_stored):
                if stored.name in seen.count:
                    act.wait_ge(stored, seen.count[stored.name])

        @block.vector
        def _(dve):
            seen, turn = Seen(), Turns()

            def use(full=True):
                b = turn()
                return (b, seen(acc_full[b])) if full else (b, None)

            def step(ins):
                ins.then_inc(dve_step, 1)
                dve.wait_ge(*seen(dve_step))

            def wide(b, rows=P):
                return acc[b][0:rows, AO:AO + T]

            dve.wait_ge(*seen(cols_turned))
            for i, n in enumerate((P, 29, 112)):
                ins = dve.tensor_copy(cols[:, i, 0:n], pt[:, i * P:i * P + n])
            ins.then_inc(cols_ready, 1)
            dve.wait_ge(*seen(cols_ready))
            dve.wait_ge(const_in, 16 * 6)
            for i in range(2):
                ins = dve.tensor_tensor(lamr[0:1, 2 * i, :], lamr[0:1, 2 * i, :], lamr[0:1, 2 * i + 1, :], ALU.mult)
            step(ins)
            dve.tensor_reduce(lamt[0:1, 0:2], lamr[0:1, 0:4:2, :], AX.X, ALU.add).then_inc(lam_sum, 1)
            dve.wait_ge(*seen(lam_exp))
            dve.scalar_tensor_tensor(out=lamt[0:1, 4:5], in0=lamt[0:1, 3:4], scalar=-L1, in1=lamt[0:1, 2:3],
                                     op0=ALU.add, op1=ALU.subtract).then_inc(lam_ready, 1)
            dve.wait_ge(*seen(lam_sent))
            dve.tensor_copy(lamt[:, NLAM:NLAM + 1], ob[0][:, 0:1]).then_inc(cols_ready, 1)
            seen(cols_ready)
            dve.tensor_scalar(lamt[:, SUBS:SUBS + 1], cols[:, 1, SUBG:SUBG + 1], 1.0 - L1, None, ALU.mult).then_inc(dve_step, 1)
            seen(dve_step)
            for t in range(QT):
                use()

            def modulation(layer):
                counts, last = MODS[kinds[layer - 1] if layer else None]
                for s, n in enumerate(counts):
                    used = seen(raw_used[s], n)
                    if s == last:
                        dve.wait_ge(*used)
                for g in range(2):
                    ins = dve.tensor_tensor(mod[:, :, g], ob[1][:, MO + g:MO + 48:2], cols[:, 0, layer * 24:layer * 24 + 24], ALU.add)
                step(ins)
                for g in range(2):
                    ins = dve.scalar_tensor_tensor(out=amul[:, :, g], in0=mod[:, KT:2 * KT, g], scalar=1.0,
                                                   in1=cols[:, 0, NORMG + layer * KT:NORMG + (layer + 1) * KT], op0=ALU.add, op1=ALU.mult)
                ins.then_inc(mod_ready, 1)

            def rest(kt):
                dve.wait_ge(*seen(ht_full))
                dve.tensor_tensor(hl[:, kt, :], ht[:, kt % 2, :], hh[:, kt, :].bitcast(F32), ALU.subtract).then_inc(h_ready, 1)

            def normalise():
                use()
                dve.wait_ge(*seen(root_ready))
                step(dve.reciprocal(rinv[:, :], rinv[:, :]))
                for kt in range(KT):
                    if kt >= 2:
                        dve.wait_ge(*seen(xr_used))
                    dve.tensor_tensor(two[:, kt % 2, :], x[:, kt, :], rinv[:, :], ALU.mult).then_inc(xr_full, 1)
                    if kt >= 1:
                        rest(kt - 1)
                seen(xr_used, 2)
                rest(KT - 1)

            def rope(src, n):
                b, full = use()
                dve.wait_ge(*full)
                dve.tensor_tensor(rinv[0:n, 0:NS], acc[b][0:n, 0:NS], cs[0:n, 1, :], ALU.mult).then_inc(rot_read, 1)
                step(dve.tensor_tensor(src[0:n, P:T], src[0:n, P:T], cs[0:n, 0, :], ALU.mult))
                dve.wait_ge(*seen(rot_read))
                dve.tensor_tensor(src[0:n, P:T], src[0:n, P:T], rinv[0:n, 0:NS], ALU.add).then_inc(qk_turned, 1)
                dve.wait_ge(*seen(qk_turned))

            def minus(out, a, high):
                return dve.tensor_tensor(out, a, high.bitcast(F32), ALU.subtract)

            def stats(k, w):
                b, full = use()
                dve.wait_ge(*full)
                dve.tensor_reduce(st[:, k % 4, 1:2], acc[b][:, AO:AO + w], AX.X, ALU.max, negate=True).then_inc(nb_ready, 1)

            def turned(slot, qt):
                n = P if qt == 0 else BM
                dve.wait_ge(*seen(pt_full))
                dve.tensor_copy(ht[:, slot, 0:n], pt[:, TO:TO + n]).then_inc(pts_dve, 1)

            def y_rest(n, factor):
                b, full = use()
                dve.wait_ge(*full)
                o = acc[b][:, TO:TO + T]
                if factor is None:
                    ins = dve.tensor_tensor(comb[:, :], o, z[:, n[1], :], ALU.mult)
                else:
                    ins = dve.scalar_tensor_tensor(out=comb[:, :], in0=o, scalar=factor, in1=z[:, n[1], :], op0=ALU.mult, op1=ALU.mult)
                ins.then_inc(yt_ready, 1)
                dve.wait_ge(*seen(yhi_ready))
                at = slice(n[0], n[0] + 1) if isinstance(n[0], int) else bass.ds(n[0], 1)
                minus(yl[:, at, :], comb[:, :].rearrange("p (a t) -> p a t", a=1), yh[:, at, :]).then_inc(y_ready, 1)

            width = lambda qt: P if qt == 0 else T

            def gqa_group(g, j=0):
                def scaled(slot, n, data, gain):
                    dve.wait_ge(*seen(nroot_ready))
                    step(dve.reciprocal(ht[0:n, slot, :], ht[0:n, slot, :]))
                    dve.scalar_tensor_tensor(out=data, in0=data, scalar=cols[0:n, 1, gain + j:gain + j + 1], in1=ht[0:n, slot, :],
                                             op0=ALU.mult, op1=ALU.mult).then_inc(qk_scaled, 1)

                for full in (False, False, True, False, True, True, False):
                    use(full)
                scaled(0, HD, kv[0:HD, 0:T], KG)
                scaled(1, P, qn[:, 0, :], QG)
                scaled(0, P, qn[:, 1, :], QG)
                rope(kv, HD)
                rope(qn[:, 0], P)
                rope(qn[:, 1], P)
                use()
                use(False)
                dve.wait_ge(*seen(hi_ready))
                minus(kst[0:HD, 0, 1, :], kv[0:HD, :], kst[0:HD, 0, 0, :])
                minus(kst[HD:P, 0, 1, :], kv[0:HD, :], kst[0:HD, 0, 0, :])
                for blk in range(2):
                    dve.wait_ge(*seen(hi_ready))
                    minus(qst[HD:P, 2 * blk, :], qn[0:HD, blk, :], qst[0:HD, 2 * blk, :])
                    ins = minus(qst[0:HD, 2 * blk + 1, :], qn[HD:P, blk, :], qst[HD:P, 2 * blk + 1, :])
                ins.then_inc(st_ready, 1)

                def output(k):
                    qt, head = steps[k]
                    step(dve.reciprocal(st[:, k % 4, 3:4], st[:, k % 4, 2:3]))
                    dve.wait_ge(*seen(ob_full[k % 2]))
                    dve.tensor_scalar(osb[:, qt, head * HD:(head + 1) * HD], ob[k % 2][:, 0:HD], st[:, k % 4, 3:4], None,
                                      ALU.mult).then_inc(ob_free[k % 2], 1)

                for blk in range(2):
                    stats(0, P)
                    stats(1, P)
                    for k in range(NST):
                        if k + 2 < NST:
                            stats(k + 2, width(steps[k + 2][0]))
                        turned(k % 2, steps[k][0])
                        if k:
                            output(k - 1)
                    output(NST - 1)
                    y_rest((g * 2 + blk, blk), None)

            def diff_head(n):
                use(False)
                use(False)
                use(False)
                rope(qn[:, 0], P)
                rope(kv, P)
                use(), use(), use()
                use(False)
                dve.wait_ge(*seen(hi_ready))
                minus(qst[HD:P, 0, :], qn[0:HD, 0, :], qst[0:HD, 0, :])
                minus(qst[0:HD, 1, :], qn[HD:P, 0, :], qst[HD:P, 1, :])
                dve.wait_ge(*seen(hi_ready))
                for m in range(2):
                    for half in (0, HD):
                        at = slice(HD * m, HD * m + HD)
                        ins = minus(kst[half:half + HD, m, 1, :], kv[at, :], kst[at, m, 0, :])
                ins.then_inc(st_ready, 1)

                def output(qt):
                    dve.wait_ge(*seen(ob_full[qt % 2]))
                    dve.tensor_scalar(osb[:, qt, :], ob[qt % 2][:, 0:P], st[:, 2 * (qt % 2), 4 + qt:5 + qt], None, ALU.mult).then_inc(osb_ready if qt == QT - 1 else ob_free[qt % 2], 1)

                stats(0, P)
                stats(1, P)
                for qt in range(QT):
                    w, k, e = width(qt), 2 * (qt % 2), (two, qn)[qt % 2]
                    if qt:
                        turned((qt - 1) % 2, qt - 1)
                    dve.wait_ge(*seen(e_ready, 2))
                    step(dve.reciprocal(st[:, k:k + 2, 4 + qt:5 + qt], st[:, k:k + 2, 2:3]))
                    step(dve.scalar_tensor_tensor(out=st[:, k + 1, 10 + qt:11 + qt], in0=st[:, k + 1, 4 + qt:5 + qt], scalar=lamt[:, NLAM:NLAM + 1],
                                                  in1=st[:, k, 2:3], op0=ALU.mult, op1=ALU.mult))
                    dve.scalar_tensor_tensor(out=comb[:, 0:w], in0=e[:, 1, 0:w], scalar=st[:, k + 1, 10 + qt:11 + qt], in1=e[:, 0, 0:w],
                                             op0=ALU.mult, op1=ALU.add).then_inc(comb_ready, 1)
                    if qt + 1 < QT:
                        stats(2 * qt + 2, T)
                        stats(2 * qt + 3, T)
                    if qt:
                        output(qt - 1)
                turned((QT - 1) % 2, QT - 1)
                output(QT - 1)
                dve.wait_ge(*seen(oroot_ready))
                step(dve.reciprocal(oss[:, 0:QT], oss[:, 0:QT]))
                for t in range(QT):
                    ins = dve.tensor_scalar(osb[:, t, :], osb[:, t, :], oss[:, t:t + 1], None, ALU.mult)
                ins.then_inc(o_scaled, 1)
                y_rest((n, 0), lamt[:, SUBS:SUBS + 1])

            def add_gated(s, n):
                b, _ = use(False)
                dve.wait_ge(*seen(proj_done[s]))
                at = slice(n, n + 1) if isinstance(n, int) else bass.ds(n, 1)
                gt = slice(n + 16, n + 17) if isinstance(n, int) else bass.ds(n + 16, 1)
                for g, (c0, c1) in enumerate(((0, P), (P, T))):
                    ins = dve.scalar_tensor_tensor(
                        out=x[:, at, c0:c1], in0=acc[b][:, AO + c0:AO + c1].rearrange("p (a t) -> p a t", a=1),
                        scalar=mod[:, gt, g], in1=x[:, at, c0:c1], op0=ALU.mult, op1=ALU.add)
                ins.then_inc(x_ready, 1)

            for layer, kind in enumerate(kinds):
                modulation(layer)
                normalise()
                if kind == "mlstm":
                    mlstm_dve(dve, seen, turn, use, step, add_gated)
                    continue
                for s, n in enumerate((8, 8, 4) if kind == "gqa" else (16, 16)):
                    seen(proj_done[s], n)
                seen.repeat(dve, *((GQ_KV, lambda g: gqa_group(g, layer // 3)) if kind == "gqa" else (KT, diff_head)))

                def outs(i):
                    for s in range(2):
                        add_gated(s, i * 2 + s)
                seen.repeat(dve, KT // 2, outs)
                dve.wait_ge(*seen(x_ready, KT))
            use()
            dve.wait_ge(*seen(root_ready))
            step(dve.reciprocal(rinv[:, :], rinv[:, :]))
            for kt in range(KT):
                ins = dve.scalar_tensor_tensor(out=x[:, kt, :], in0=x[:, kt, :], scalar=cols[:, 1, FING + kt:FING + kt + 1],
                                               in1=rinv[:, :], op0=ALU.mult, op1=ALU.mult)
            ins.then_inc(normed, 1)


def row_parts(rows, A):
    v = lambda a, pat="(b p) -> b p": a.rearrange(pat, p=P)
    parts = [(rows[0:96, 0, :], v(A["b_mod"], "l (b p) -> (l b) p")),
             (rows[96:128, 0, :], v(A["norm_g"], "l (b p) -> (l b) p")),
             (rows[0:8, 1, :], v(A["c_ctx"])),
             (rows[8:16, 1, :], v(A["c"][0])),
             (rows[16:24, 1, :], v(A["final_norm_g"]))]
    for i, name in ((24, "gqa_q_norm_g"), (26, "gqa_k_norm_g")):
        parts += [(rows[i:i + 2, 1, h * HD:(h + 1) * HD], A[name]) for h in range(2)]
    parts += [(rows[28:29, 1, :], A["diff_subln_g"]),
              (rows[0:16, 2, :], v(A["mlstm_conv_b"][0])),
              (rows[16:80, 2, :], v(A["mlstm_conv_w"][0], "k (b p) -> (k b) p")),
              (rows[80:96, 2, :], v(A["mlstm_mh_norm_g"][0])),
              (rows[96:112, 2, :], v(A["mlstm_skip"][0]))]
    return parts


def constants():
    ident = np.eye(P, dtype=np.float32)
    half = np.kron(np.eye(2), np.ones((HD, HD))).astype(np.float32)
    perm = np.zeros((P, P), np.float32)
    for m in range(P):
        d = m % HD
        perm[m + HD // 2 if d < HD // 2 else m - HD // 2, m] = -1.0 if d < HD // 2 else 1.0
    tok = np.arange(NS)
    inv = (np.float32(10000.0) ** (-np.arange(HD // 4, dtype=np.float32) / np.float32(HD // 4))).astype(np.float32)
    row, col = (tok // 64).astype(np.float32), (tok % 64).astype(np.float32)
    ang = np.concatenate([row[:, None] * inv, col[:, None] * inv], axis=-1)
    table = lambda f: np.tile(f(ang).astype(np.float32).T, (P // (HD // 2), 1))
    place = np.zeros((P, P), np.float32)
    for h in range(MH):
        for d in range(2):
            place[8 * d + h, 32 * d + h] = place[8 * d + MH + h, 64 + 32 * d + h] = 1.0
    head4 = np.kron(np.eye(P // 4), np.ones((4, 4))).astype(np.float32)
    s, t = np.mgrid[0:P, 0:P]
    masks = [(1e30 * late).astype(np.float32) for late in (t < s, t > s)]
    return np.concatenate([ident, np.ones((P, P), np.float32), half, perm, table(np.cos), table(np.sin),
                           place, head4, *masks], axis=1)


_OUTS = {"y_prompt": (1, NP_, D), "y_sample": (1, NS, D), "gqa_k": (1, 2, NP_, GQ_KV, HD), "gqa_v": (1, 2, NP_, GQ_KV, HD),
         "diff_k": (1, 1, NP_, 8, 2, HD), "diff_v": (1, 1, NP_, 8, P),
         "mlstm_C": (1, 1, 2, MH, MD, MD), "mlstm_n": (1, 1, 2, MH, MD), "mlstm_m": (1, 1, 2, MH)}


def kernel(**inputs):
    import concourse.bacc as _bacc
    from concourse.bass_utils import run_bass_kernel_spmd as _run

    nc = _bacc.Bacc("TRN2", target_bir_lowering=False, num_devices=1)
    arrays, A = {}, {}
    for name, a in {**inputs, "consts": constants()}.items():
        arrays[f"in_{name}"] = a = np.ascontiguousarray(a)
        A[name] = nc.dram_tensor(f"in_{name}", a.shape, mybir.dt.from_np(a.dtype), kind="ExternalInput").ap()
    O = {n: nc.dram_tensor(f"out_{n}", s, F32, kind="ExternalOutput").ap() for n, s in _OUTS.items()}
    scratch = {n: nc.dram_tensor(f"scratch_{n}", s, F32, kind="Internal").ap()
               for n, s in (("xm", (MH, MB, P, T + 5)), ("xc", (MH, MB, P, T)), ("y", (MH * MB, P, T)))}
    build(nc, A, O, scratch)
    r = _run(nc, [arrays], core_ids=[0])
    return tuple(r.results[0][f"out_{n}"] for n in _OUTS)
```
